# Optimizing a Trainium2 kernel written in Bass

```python
import jax, jax.numpy as jnp
from jax import lax
import numpy as np

D_MODEL = 1024
BATCH = 1
SEQ = 256
DEPTH = 1
DEC_BATCH = 8
DEC_SEQ = 16
PAST_LEN = 512

CHUNK = 64
D_CONV_A = D_MODEL
D_CONV_B = D_MODEL
K_A = 3
K_B = 31
N_GROUPS = 4
EXPERTS_PER_GROUP = 8
N_EXPERTS = N_GROUPS * EXPERTS_PER_GROUP
TOP_K_IN_GROUP = 2
D_EXPERT = D_MODEL // 2
RMS_EPS = 1e-6
LN_EPS = 1e-5
SPLITS = (D_CONV_A, 2 * D_CONV_A, 3 * D_CONV_A, 3 * D_CONV_A + D_CONV_B, 3 * D_CONV_A + 2 * D_CONV_B)
IN_COLS = 3 * D_CONV_A + 2 * D_CONV_B + 2 * D_MODEL

kernel_name = "hybrid_shortconv_conformer_hmoe_stream_step"

def rms_norm(x, g):
    x32 = x.astype(jnp.float32)
    y = x32 * lax.rsqrt(jnp.mean(x32 * x32, axis=-1, keepdims=True) + RMS_EPS)
    return y.astype(x.dtype) * g

def layer_norm(x, g, b):
    x32 = x.astype(jnp.float32)
    mu = jnp.mean(x32, axis=-1, keepdims=True)
    xc = x32 - mu
    var = jnp.mean(xc * xc, axis=-1, keepdims=True)
    return (xc * lax.rsqrt(var + LN_EPS)).astype(x.dtype) * g + b

def causal_depthwise_conv(u, buf, w):
    k = w.shape[0]
    full = jnp.concatenate([buf.astype(u.dtype), u], axis=1)
    y = lax.conv_general_dilated(full, w[:, None, :].astype(u.dtype), window_strides=(1,), padding='VALID',
                                 dimension_numbers=('NWC', 'WIO', 'NWC'), feature_group_count=u.shape[-1])
    return y, full[:, full.shape[1] - (k - 1):, :]

def mixer_block(x, buf_a, buf_b, norm1_g, w_in, gate_b, conv_a_w, w_out_a,
                conv_b_w, conv_b_b, ln_b_g, ln_b_b, w_out_b, b_out_b, w_o):
    xn = rms_norm(x, norm1_g)
    proj = jnp.einsum('btd,dc->btc', xn, w_in)
    b_a, c_a, h_a, glu_a, glu_b, g_in = jnp.split(proj, SPLITS, axis=-1)
    conv_a, new_a = causal_depthwise_conv(c_a * h_a, buf_a, conv_a_w)
    y_a = jnp.einsum('btc,cd->btd', b_a * conv_a, w_out_a)
    u_b = glu_a * jax.nn.sigmoid(glu_b)
    conv_b, new_b = causal_depthwise_conv(u_b, buf_b, conv_b_w)
    v_b = jax.nn.silu(layer_norm(conv_b + conv_b_b, ln_b_g, ln_b_b))
    y_b = jnp.einsum('btc,cd->btd', v_b, w_out_b) + b_out_b
    g_a, g_b = jnp.split(jax.nn.sigmoid(g_in + gate_b), 2, axis=-1)
    out = jnp.einsum('btd,de->bte', g_a * y_a + g_b * y_b, w_o)
    return x + out, new_a, new_b

def hier_moe(x, norm2_g, rg_w, rg_b, re_w, re_b, w_gate, w_up, w_down):
    bsz, t, d = x.shape
    xn = rms_norm(x, norm2_g).reshape(bsz * t, d)
    lg = jnp.einsum('nd,dg->ng', xn, rg_w).astype(jnp.float32) + rg_b.astype(jnp.float32)
    p_group = jax.nn.softmax(lg, axis=-1)
    p_top, grp = lax.top_k(p_group, 1)
    le = (jnp.einsum('nd,de->ne', xn, re_w).astype(jnp.float32) + re_b.astype(jnp.float32))
    le = le.reshape(-1, N_GROUPS, EXPERTS_PER_GROUP)
    le_sel = jnp.take_along_axis(le, grp[:, :, None], axis=1)[:, 0]
    top_l, top_i = lax.top_k(le_sel, TOP_K_IN_GROUP)
    w_top = jax.nn.softmax(top_l, axis=-1) * p_top
    expert_id = grp * EXPERTS_PER_GROUP + top_i
    combine = jnp.sum(jax.nn.one_hot(expert_id, N_EXPERTS, dtype=jnp.float32) * w_top[..., None], axis=1)
    combine = combine.astype(x.dtype)
    out = jnp.zeros_like(xn)
    for e in range(N_EXPERTS):
        hdn = jax.nn.silu(xn @ w_gate[e]) * (xn @ w_up[e])
        out = out + combine[:, e:e + 1] * (hdn @ w_down[e])
    return x + out.reshape(bsz, t, d)

def trunk(x, bufs_a, bufs_b, norm1_g, w_in, gate_b, conv_a_w, w_out_a, conv_b_w, conv_b_b,
          ln_b_g, ln_b_b, w_out_b, b_out_b, w_o, norm2_g, router_group_w, router_group_b,
          router_expert_w, router_expert_b, exp_w_gate, exp_w_up, exp_w_down, final_norm_g):
    new_a, new_b = [], []
    for l in range(DEPTH):
        x, na, nb = mixer_block(x, bufs_a[l], bufs_b[l], norm1_g[l], w_in[l], gate_b[l], conv_a_w[l],
                                w_out_a[l], conv_b_w[l], conv_b_b[l], ln_b_g[l], ln_b_b[l],
                                w_out_b[l], b_out_b[l], w_o[l])
        x = hier_moe(x, norm2_g[l], router_group_w[l], router_group_b[l], router_expert_w[l],
                     router_expert_b[l], exp_w_gate[l], exp_w_up[l], exp_w_down[l])
        new_a.append(na)
        new_b.append(nb)
    return rms_norm(x, final_norm_g), jnp.stack(new_a), jnp.stack(new_b)

def setup_inputs(seed: int = 0) -> dict:
    key = jax.random.key(seed)
    ks = jax.random.split(key, 32)
    f32 = jnp.float32
    nrm = lambda k, shape, s: jax.random.normal(k, shape, f32) * s
    L = DEPTH
    return {
        "x_prompt": nrm(ks[0], (BATCH, SEQ, D_MODEL), 1.0),
        "x_sample": nrm(ks[1], (DEC_BATCH, DEC_SEQ, D_MODEL), 1.0),
        "cache_conv_a": nrm(ks[2], (L, DEC_BATCH, K_A - 1, D_CONV_A), 1.0),
        "cache_conv_b": nrm(ks[3], (L, DEC_BATCH, K_B - 1, D_CONV_B), 1.0),
        "norm1_g": 1.0 + nrm(ks[4], (L, D_MODEL), 0.02),
        "w_in": nrm(ks[5], (L, D_MODEL, IN_COLS), D_MODEL ** -0.5),
        "gate_b": nrm(ks[6], (L, 2 * D_MODEL), 0.02),
        "conv_a_w": nrm(ks[7], (L, K_A, D_CONV_A), K_A ** -0.5),
        "w_out_a": nrm(ks[8], (L, D_CONV_A, D_MODEL), D_CONV_A ** -0.5),
        "conv_b_w": nrm(ks[9], (L, K_B, D_CONV_B), K_B ** -0.5),
        "conv_b_b": nrm(ks[10], (L, D_CONV_B), 0.02),
        "ln_b_g": 1.0 + nrm(ks[11], (L, D_CONV_B), 0.02),
        "ln_b_b": nrm(ks[12], (L, D_CONV_B), 0.02),
        "w_out_b": nrm(ks[13], (L, D_CONV_B, D_MODEL), D_CONV_B ** -0.5),
        "b_out_b": nrm(ks[14], (L, D_MODEL), 0.02),
        "w_o": nrm(ks[15], (L, D_MODEL, D_MODEL), D_MODEL ** -0.5),
        "norm2_g": 1.0 + nrm(ks[16], (L, D_MODEL), 0.02),
        "router_group_w": nrm(ks[17], (L, D_MODEL, N_GROUPS), D_MODEL ** -0.5),
        "router_group_b": nrm(ks[18], (L, N_GROUPS), 0.01),
        "router_expert_w": nrm(ks[19], (L, D_MODEL, N_EXPERTS), D_MODEL ** -0.5),
        "router_expert_b": nrm(ks[20], (L, N_EXPERTS), 0.01),
        "exp_w_gate": nrm(ks[21], (L, N_EXPERTS, D_MODEL, D_EXPERT), D_MODEL ** -0.5),
        "exp_w_up": nrm(ks[22], (L, N_EXPERTS, D_MODEL, D_EXPERT), D_MODEL ** -0.5),
        "exp_w_down": nrm(ks[23], (L, N_EXPERTS, D_EXPERT, D_MODEL), D_EXPERT ** -0.5),
        "final_norm_g": 1.0 + nrm(ks[24], (D_MODEL,), 0.02),
    }

def reference(x_prompt, x_sample, cache_conv_a, cache_conv_b, norm1_g, w_in, gate_b, conv_a_w, w_out_a,
              conv_b_w, conv_b_b, ln_b_g, ln_b_b, w_out_b, b_out_b, w_o, norm2_g, router_group_w,
              router_group_b, router_expert_w, router_expert_b, exp_w_gate, exp_w_up, exp_w_down,
              final_norm_g):
    weights = (norm1_g, w_in, gate_b, conv_a_w, w_out_a, conv_b_w, conv_b_b, ln_b_g, ln_b_b, w_out_b,
               b_out_b, w_o, norm2_g, router_group_w, router_group_b, router_expert_w, router_expert_b,
               exp_w_gate, exp_w_up, exp_w_down, final_norm_g)
    bsz = x_prompt.shape[0]
    zeros_a = jnp.zeros((DEPTH, bsz, K_A - 1, D_CONV_A), x_prompt.dtype)
    zeros_b = jnp.zeros((DEPTH, bsz, K_B - 1, D_CONV_B), x_prompt.dtype)
    y_prompt, new_a_prompt, new_b_prompt = trunk(x_prompt, zeros_a, zeros_b, *weights)
    y_sample, new_a_sample, new_b_sample = trunk(x_sample, cache_conv_a, cache_conv_b, *weights)
    return (y_prompt, y_sample, new_a_prompt, new_a_sample, new_b_prompt, new_b_sample)


_drawn_inputs = setup_inputs


def setup_inputs(seed=0):
    import zlib

    import numpy as np

    out = dict(_drawn_inputs(seed))
    spreads = {}
    factors = {'gate_b': 4.36,
     'ln_b_g': 10.735,
     'ln_b_b': 4.188,
     'b_out_b': 3.543,
     'router_group_b': 14.795,
     'router_expert_b': 11.376,
     'final_norm_g': 8.146,
     'norm2_g': 2.94}
    for name, (base, spread) in spreads.items():
        noise = np.random.default_rng([zlib.crc32(name.encode()), seed]).standard_normal(out[name].shape)
        drawn = base * np.exp(spread * noise) if base else spread * noise
        out[name] = __import__('jax').numpy.asarray(drawn.astype(out[name].dtype))
    for name, factor in factors.items():
        out[name] = (out[name] * factor).astype(out[name].dtype)
    return out
```

```python
from contextlib import ExitStack

import concourse.bass as bass
from concourse import mybir

F32 = mybir.dt.float32
I32 = mybir.dt.int32
U32 = mybir.dt.uint32
BF16 = mybir.dt.bfloat16
ALU = mybir.AluOpType
ACT = mybir.ActivationFunctionType
AX = mybir.AxisListType

P = 128


def trunk_program(nc, x_prompt, x_sample, cache_a, cache_b, norm1_g, w_in, gate_b, conv_a_w, w_out_a, conv_b_w,
                  conv_b_b, ln_b_g, ln_b_b, w_out_b, b_out_b, w_o, norm2_g, group_w, group_b, expert_w, expert_b,
                  w_gate, w_up, w_down, final_g, y_prompt, y_sample, new_a_prompt, new_a_sample, new_b_prompt,
                  new_b_sample):
    D = x_prompt.shape[2]
    NP = x_prompt.shape[1]
    NS, TS = x_sample.shape[0], x_sample.shape[1]
    N = NP + NS * TS
    NT = N // P
    KB = D // P
    KA_TAPS, KB_TAPS = conv_a_w.shape[1], conv_b_w.shape[1]
    HA, HB = KA_TAPS - 1, KB_TAPS - 1
    NE, DE = w_gate.shape[1], w_gate.shape[3]
    NG = group_w.shape[2]
    EPG = NE // NG
    HK = DE // P
    T = 64
    HALF = 512
    RING = 6
    MAX_ITEMS = NE + 2 * N // T
    R = NG + NE
    BIG = 1.0e30

    PA = HA + NP
    SA = HA + TS
    PB, SB = HB + NP, HB + TS
    WA, WB = PA + NS * SA, PB + NS * SB

    SECTION = {"B": 0, "C": 1, "H": 2, "GA": 3, "GB": 4, "gA": 5, "gB": 6}
    CHUNKS = [("GB", 0), ("GA", 0), ("GB", 1), ("GA", 1), ("C", 0), ("H", 0), ("C", 1), ("H", 1), ("B", 0),
              ("B", 1), ("Wa", 0), ("Wa", 1), ("gA", 0), ("gA", 1), ("gB", 0), ("gB", 1), ("Wb", 0), ("Wb", 1),
              ("Wo", 0), ("Wo", 1)]
    NCH = len(CHUNKS)
    GROUPS = []
    for q, (s, half) in enumerate(CHUNKS):
        for j in range(NT if s == "Wo" else HALF // P):
            GROUPS.append((s, j if s == "Wo" else half * (HALF // P) + j, q))
    BY_ACT = ("GB", "C", "Wa", "gA", "gB")
    CHUNK_END = [1 + max(i for i, x in enumerate(GROUPS) if x[2] == q) for q in range(NCH)]
    NBANK = 4

    def group(s, m):
        return [i for i, x in enumerate(GROUPS) if x[0] == s and x[1] == m][0]

    AUX = [("vec", 0, "dve")]
    AUX += [("xT", k, "act" if k % 2 else "dve") for k in range(KB)]
    AUX += [("ca", 0, "dve")]
    AUX += [("cb", j, "act") for j in range(4)]
    OUT_TILES = ["ap", "as", "bp", "bs0", "bs1"]
    AUX += [("new", j, "act") for j in range(2 * len(OUT_TILES))]
    AUX += [("mean", 0, "dve"), ("var", 0, "dve")]
    AUX += [("x2T", k, "act" if k % 2 else "dve") for k in range(KB)]
    AUX += [("logit", 0, "dve"), ("pos", 0, "dve"), ("table", 0, "dve")]

    def aux(name, j=0):
        return AUX.index([a for a in AUX if a[0] == name and a[1] == j][0])

    V_N1, V_GATE, V_CA, V_CB = 0, 1, 3, 3 + KA_TAPS
    V_CBB = V_CB + KB_TAPS
    V_LNG, V_LNB, V_BO = V_CBB + 1, V_CBB + 2, V_CBB + 3
    NV = V_BO + 1

    y_rows = nc.dram_tensor("expert_rows", (MAX_ITEMS * T, D), F32, kind="Internal").ap()

    with ExitStack() as ctx:
        def sb(name, shape, dt=F32):
            return ctx.enter_context(nc.sbuf_tensor(name, shape, dt))

        def sem(name):
            return ctx.enter_context(nc.semaphore(name))

        bank = [ctx.enter_context(nc.psum_tensor(f"bank{i}", [P, 512], F32)) for i in range(8)]
        ring = [sb(f"ring{i}", [P, 4096]) for i in range(RING)]
        x_tok = sb("x_tok", [P, NT, D])
        n_tok = sb("n_tok", [P, NT, D])
        merged = n_tok[:, :, :].rearrange("p t d -> p (t d)").rearrange("p (k n) -> p k n", n=N)
        tails = n_tok[:, :, :].rearrange("p t d -> p (t d)")[:, 0:KB * NS * (HA + HB)].rearrange(
            "p (k n) -> p k n", k=KB)
        xT = sb("xT", [P, KB, N])
        ua = sb("ua", [P, KB * WA])
        ub = sb("ub", [P, KB * WB])
        cvb = sb("cvb", [P, KB, N])
        cva = sb("cva", [P, KB, N])
        tmp = sb("tmp", [P, HALF // P, N])
        stage = sb("stage", [P, 2, D])
        vec = sb("vec", [P, KB, NV])
        ident = sb("ident", [P, P])
        ones = sb("ones", [P, P])
        before = sb("before", [P, P])
        iota = sb("iota", [P, T])
        small = sb("small", [P, 48])
        rbias = sb("rbias", [P, R])[:, :]
        down_rank = sb("down_rank", [P, NE])[:, :]
        table = sb("table", [1, 2 * NE + 1], I32)

        ua_k = ua[:, :].rearrange("p (k n) -> p k n", k=KB)
        ub_k = ub[:, :].rearrange("p (k n) -> p k n", k=KB)

        def ua_new(m, tap):
            s = ua_k[:, m, PA:WA].rearrange("p (s n) -> p s n", s=NS)
            return ua_k[:, m, tap:tap + NP], s[:, :, tap:tap + TS]

        def ub_new(m, tap):
            s = ub_k[:, m, PB:WB].rearrange("p (s n) -> p s n", s=NS)
            return ub_k[:, m, tap:tap + NP], s[:, :, tap:tap + TS]

        def both(t):
            return t[:, 0:NP], t[:, NP:N].rearrange("p (s n) -> p s n", s=NS)

        sq = ua[:, 0:KB * N].rearrange("p (k n) -> p k n", k=KB)
        g2 = ub[:, 0:D]
        gf = ub[:, D:2 * D]
        junk = ub[:, 2 * D:3 * D]
        rw = ub[:, 3 * D:3 * D + KB * R].rearrange("p (k r) -> p k r", k=KB)
        ua_b, cva_b = ua[:, :].bitcast(BF16), cva[:, :, :].rearrange("p k n -> p (k n)").bitcast(BF16)
        parts = [x.rearrange("p (i d) -> p i d", d=D) for x in
                 (ua_b[:, 0:NT * D], ua_b[:, NT * D:2 * NT * D], cva_b[:, 0:NT * D])]
        pick = cvb[:, 0, 0:NT * T // 2].bitcast(BF16).rearrange("p (i t) -> p i t", i=NT)
        xe = cvb[:, 1:3, :].rearrange("p k n -> p (k n)")[:, 0:KB * T].rearrange("p (k t) -> p k t", k=KB)
        sig = cvb[:, 3:5, :].rearrange("p k n -> p (k n)")[T:2 * T, 0:DE]
        hid = cvb[:, 5:7, :].rearrange("p k n -> p (k n)")[0:T, 0:DE]
        hidT = cvb[:, 7, 0:HK * T].rearrange("p (k t) -> p k t", k=HK)
        y_half = stage[:, 0, 0:HALF]
        rowsA = xT[:, :, :].rearrange("p k n -> p (k n)").rearrange("p (i d) -> p i d", d=D)
        rowsB = cva[:, :, :].rearrange("p k n -> p (k n)").rearrange("p (i d) -> p i d", d=D)
        rt = tmp[:, :, :].rearrange("p k n -> p (k n)")
        cols = [0]

        def scratch(n, rows=P):
            a = rt[0:rows, cols[0]:cols[0] + n]
            cols[0] += n
            return a

        x_in = sem("x_in")
        vec_in = sem("vec_in")
        cache_in = sem("cache_in")
        rw_in = sem("rw_in")
        g_in = sem("g_in")
        weights_in = [sem(f"weights_in{i}") for i in range(RING)]
        consts = sem("consts")
        hist_zero = sem("hist_zero")
        ssq_ready = sem("ssq_ready")
        root_in = sem("root_in")
        root_out = sem("root_out")
        normed = sem("normed")
        grp_done = sem("grp_done")
        act_grp = sem("act_grp")
        dve_grp = sem("dve_grp")
        aux_done = sem("aux_done")
        act_aux = sem("act_aux")
        dve_aux = sem("dve_aux")
        conv_b_ops = sem("conv_b_ops")
        conv_a_ops = sem("conv_a_ops")
        dve_chain = sem("dve_chain")
        centred = sem("centred")
        squared = sem("squared")
        scaled = sem("scaled")
        v_ready = sem("v_ready")
        gate_a_merged = sem("gate_a_merged")
        gate_b_merged = sem("gate_b_merged")
        stage_out = [sem(f"stage_out{i}") for i in range(2)]
        tails_ready = sem("tails_ready")
        masks_ready = sem("masks_ready")
        exp_in = sem("exp_in")
        exp_out = sem("exp_out")
        counts_ready = sem("counts_ready")
        tables_ready = sem("tables_ready")
        picked = sem("picked")
        pick_half = sem("pick_half")
        rem_ready = sem("rem_ready")
        gathered = sem("gathered")
        xe_ready = sem("xe_ready")
        gate_up_done = sem("gate_up_done")
        hid_turned = sem("hid_turned")
        hidT_ready = sem("hidT_ready")
        part_ready = [sem(f"part{i}_ready") for i in range(3)]
        rest_ready = sem("rest_ready")
        blank_zero = sem("blank_zero")
        sig_ready = sem("sig_ready")
        hid_ready = sem("hid_ready")
        down_done = sem("down_done")
        y_ready = sem("y_ready")
        y_stored = [sem(f"y_stored{i}") for i in range(2)]
        slots_ready = sem("slots_ready")
        all_stored = sem("all_stored")
        rows_in = [sem(f"rows_in{i}") for i in range(2 * NT)]
        final_ready = sem("final_ready")
        y_out = sem("y_out")

        def wait_group_read(eng, g):
            by_act = GROUPS[g][0] in BY_ACT
            n = sum((x[0] in BY_ACT) == by_act for x in GROUPS[:g + 1])
            eng.wait_ge(act_grp if by_act else dve_grp, n)

        def wait_aux_read(eng, a):
            n = sum(x[2] == AUX[a][2] for x in AUX[:a + 1])
            eng.wait_ge(act_aux if AUX[a][2] == "act" else dve_aux, n)

        def slot_fill(q):
            return q % RING, 16 * (q // RING + 1)

        w_in_k = w_in.rearrange("l (k p) c -> p (l k) c", p=P)
        w_sq = {"Wa": w_out_a.rearrange("l (k p) c -> p (l k) c", p=P),
                "Wb": w_out_b.rearrange("l (k p) c -> p (l k) c", p=P),
                "Wo": w_o.rearrange("l (k p) c -> p (l k) c", p=P)}
        w_gu = {0: w_gate.rearrange("l e (k p) c -> (l e) p k c", p=P), 1: w_up.rearrange("l e (k p) c -> (l e) p k c", p=P)}
        w_dn = w_down.rearrange("l e (k p) c -> (l e) p k c", p=P)

        def wide(slot):
            return ring[slot][:, :].rearrange("p (k c) -> p k c", k=KB)

        def deep(slot):
            return ring[slot][:, :].rearrange("p (k c) -> p k c", k=HK)

        lg = scratch(NT * R).rearrange("p (i r) -> p i r", i=NT)
        gmax = scratch(NT)
        ghot = scratch(NT * NG).rearrange("p (i g) -> p i g", i=NT)
        gexp = scratch(NT * NG).rearrange("p (i g) -> p i g", i=NT)
        le = scratch(NT * NE).rearrange("p (i e) -> p i e", i=NT)
        hot = [scratch(NT * NE).rearrange("p (i e) -> p i e", i=NT) for _ in range(2)]
        t0 = scratch(NT * NE).rearrange("p (i e) -> p i e", i=NT)
        t1 = scratch(NT * NE).rearrange("p (i e) -> p i e", i=NT)
        both_hot = scratch(NT * NE).rearrange("p (i e) -> p i e", i=NT)
        top = [scratch(NT) for _ in range(2)]
        dexp = scratch(NT)
        coef = [scratch(NT) for _ in range(2)]
        psum_g = scratch(NT)
        slot_f = [scratch(NT) for _ in range(2)]
        slot_rem = scratch(2 * NT).rearrange("p (c i) -> p c i", c=2)
        slot_u32 = [scratch(NT).bitcast(U32) for _ in range(2)]
        cnt = scratch(1, NE)
        ntile = scratch(1, NE)
        ntile_b = scratch(P, NE)
        prefix = scratch(2 * NE + 1, NE)
        base_slot = scratch(NE)
        assert cols[0] <= 4 * N

        OUT_ROWS = [HA, NS * HA, HB, NS // 2 * HB, NS // 2 * HB]
        nbs = new_b_sample.rearrange("l s h d -> (l s h) d")
        OUT_DST = [new_a_prompt.rearrange("l b h d -> (l b h) d"), new_a_sample.rearrange("l s h d -> (l s h) d"),
                   new_b_prompt.rearrange("l b h d -> (l b h) d"), nbs[0:NS // 2 * HB, :], nbs[NS // 2 * HB:, :]]
        ACT_AUX_NEW = sum(x[2] == "act" for x in AUX[:aux("mean")])
        WO_LAST = [[i for i, x in enumerate(GROUPS) if x == ("Wo", t, NCH - 1)][0] for t in range(NT)]
        XE = bank[0][:, 0:KB * T]
        G, U = bank[1][0:T, :], bank[1][T:2 * T, :]
        HT = bank[2][:, 0:HK * T]
        Y = bank[3]

        block = ctx.enter_context(nc.Block())

        @block.sync
        def _(sp):
            sp.dma_start(x_tok[:, 0:NP // P, :], x_prompt[0].rearrange("(i p) d -> p i d", p=P)).then_inc(x_in, 16)
            sp.dma_start(x_tok[:, NP // P, :], x_sample.rearrange("s t d -> (s t) d")).then_inc(x_in, 16)
            sp.wait_ge(vec_in, 16 * 8)
            for q, (s, half) in enumerate(CHUNKS):
                if q >= RING:
                    sp.wait_ge(grp_done, CHUNK_END[q - RING])
                src = w_sq[s][:, :, half * HALF:(half + 1) * HALF] if s in w_sq else \
                    w_in_k[:, :, SECTION[s] * D + half * HALF:SECTION[s] * D + (half + 1) * HALF]
                sp.dma_start(wide(q % RING), src).then_inc(weights_in[q % RING], 16)

            def expert_weights(e, par, first):
                for c in range(3):
                    q = NCH + 3 * par + c
                    if first:
                        sp.wait_ge(grp_done, CHUNK_END[q - RING])
                    else:
                        sp.wait_ge([gate_up_done, gate_up_done, down_done][c], last_item)
                    dst, src = (deep(q % RING), w_dn) if c == 2 else (wide(q % RING), w_gu[c])
                    sp.dma_start(dst, src[e, :, :, :] if first else
                                 src[bass.ds(e, 1), :, :, :].rearrange("e p k c -> p (e k) c"))\
                      .then_inc(weights_in[q % RING], 16)

            expert_weights(0, 0, True)
            expert_weights(1, 1, True)
            sp.wait_ge(tables_ready, 1)
            with sp.Fori(1, NE // 2) as pair:
                for par in range(2):
                    last_item = sp.value_load(table[0:1, bass.ds(pair * 2 + (NE + par - 1), 1)], min_val=1, max_val=MAX_ITEMS)
                    expert_weights(pair * 2 + par, par, False)

        @block.gpsimd
        def _(pool):
            pool.memset(ident[:], 0.0).then_inc(consts, 1)
            pool.memset(ones[:], 1.0).then_inc(consts, 1)
            pool.wait_ge(consts, 2)
            pool.affine_select(out=ident[:], in_=ident[:], pattern=[[1, P]], compare_op=ALU.not_equal, fill=1.0,
                               base=0, channel_multiplier=-1).then_inc(consts, 1)
            pool.affine_select(out=before[:], in_=ones[:], pattern=[[1, P]], compare_op=ALU.is_gt, fill=0.0,
                               base=0, channel_multiplier=-1).then_inc(consts, 1)
            pool.iota(iota[:], pattern=[[1, T]], base=0, channel_multiplier=0,
                      allow_small_or_imprecise_dtypes=True).then_inc(consts, 1)
            pool.iota(down_rank, pattern=[[-1, NE]], base=NE, channel_multiplier=0,
                      allow_small_or_imprecise_dtypes=True).then_inc(consts, 1)
            pool.memset(ua_k[:, :, 0:HA], 0.0).then_inc(hist_zero, 1)
            pool.memset(ub_k[:, :, 0:HB], 0.0).then_inc(hist_zero, 1)
            for a in (aux("xT", KB - 2), aux("xT", KB - 1)):
                wait_aux_read(pool, a)
            pool.memset(n_tok[:, NT - 1, :], 0.0).then_inc(blank_zero, 1)
            wait_group_read(pool, group("GA", KB - 1))
            pool.wait_ge(blank_zero, 1)
            for h in range(2):
                pool.dma_start(
                    y_rows[NE * T:MAX_ITEMS * T, h * HALF:(h + 1) * HALF].rearrange("(a p) d -> p a d", p=P),
                    n_tok[:, NT - 1, 0:HALF].unsqueeze(1).to_broadcast([P, (MAX_ITEMS - NE) * T // P, HALF]))\
                    .then_inc(y_stored[h], 16)
            wait_group_read(pool, group("H", KB - 1))
            for m in range(KB):
                for src, first, last_col, h in ((ua_k[:, m, PA:WA], 0, SA, HA), (ub_k[:, m, PB:WB], NS * HA, SB, HB)):
                    pool.tensor_copy(tails[:, m, first:first + NS * h].rearrange("p (s n) -> p s n", s=NS),
                                     src.rearrange("p (s n) -> p s n", s=NS)[:, :, last_col - h:last_col])\
                        .then_inc(tails_ready, 1)
            for m in range(KB):
                wait_group_read(pool, group("Wa", m))
                wait_group_read(pool, group("gA", m))
                pool.tensor_tensor(merged[:, m, :], merged[:, m, :], tmp[:, m % 4, :], ALU.mult)\
                    .then_inc(gate_a_merged, 1)
            for m in range(KB):
                pool.wait_ge(gate_a_merged, m + 1)
                wait_group_read(pool, group("Wb", m))
                pool.tensor_tensor(merged[:, m, :], merged[:, m, :], cva[:, m, :], ALU.add).then_inc(gate_b_merged, 1)
            for i in range(NT):
                pool.wait_ge(part_ready[0], i + 1)
                pool.tensor_tensor(n_tok[:, i, :], n_tok[:, i, :], parts[0][:, i, :], ALU.subtract)\
                    .then_inc(rest_ready, 1)
            for i in range(NT):
                pool.wait_ge(part_ready[1], i + 1)
                pool.tensor_tensor(parts[2][:, i, :], n_tok[:, i, :], parts[1][:, i, :], ALU.subtract)\
                    .then_inc(part_ready[2], 1)
            pool.wait_ge(tables_ready, 1)
            for h in range(2):
                pool.wait_ge(y_stored[h], 16)
            items = pool.value_load(table[0:1, 2 * NE:2 * NE + 1], min_val=NE, max_val=MAX_ITEMS)
            with pool.Fori(0, items) as i:
                pool.wait_ge(y_ready, i + 1)
                for h in range(2):
                    pool.dma_start(y_rows[bass.ds(i * T, T), h * HALF:(h + 1) * HALF], y_half[h * T:(h + 1) * T, :])\
                        .then_inc(y_stored[h], 16)
            pool.wait_ge(slots_ready, 1)
            pool.wait_ge(all_stored, 1)
            for i in range(NT):
                for c in range(2):
                    pool.indirect_dma_start(
                        out=(rowsA if c == 0 else rowsB)[:, i, :], out_offset=None, in_=y_rows,
                        in_offset=bass.IndirectOffsetOnAxis(ap=slot_u32[c][:, i:i + 1], axis=0))\
                        .then_inc(rows_in[2 * i + c], 16)

        @block.scalar
        def _(act):
            rows = [(V_N1, norm1_g), (V_GATE, gate_b.rearrange("l (a d) -> (l a) d", d=D)),
                    (V_CA, conv_a_w.rearrange("l k d -> (l k) d")), (V_CB, conv_b_w.rearrange("l k d -> (l k) d")),
                    (V_CBB, conv_b_b), (V_LNG, ln_b_g), (V_LNB, ln_b_b), (V_BO, b_out_b)]
            for r, src in rows:
                act.dma_start(stage[r:r + src.shape[0], 0, :], src).then_inc(vec_in, 16)
            act.wait_ge(x_in, 32)
            for i in range(NT):
                act.activation(cva[:, :, :].rearrange("p k n -> p (k n)")[:, i * D:(i + 1) * D], x_tok[:, i, :],
                               ACT.Square, accum_out=small[:, i:i + 1]).then_inc(ssq_ready, 1)
            act.wait_ge(root_in, 1)
            act.activation(small[:, 8:8 + NT], small[:, 4:4 + NT], ACT.Sqrt).then_inc(root_out, 1)

            def read_aux(a):
                name, j, eng = AUX[a]
                if eng != "act":
                    return
                b = bank[4 + a % 4]
                act.wait_ge(aux_done, a + 1)
                if name == "xT":
                    act.wait_ge(dve_aux, 1)
                    act.activation(xT[:, j, :], b[:, 0:N], ACT.Copy, scale=vec[:, j, V_N1:V_N1 + 1])\
                       .then_inc(act_aux, 1)
                elif name == "cb":
                    t, mh = j // 2, j % 2
                    for m in range(4):
                        dst = ub_k[:, 4 * mh + m, PB:WB].rearrange("p (s n) -> p s n", s=NS)[
                            :, 4 * t:4 * t + 4, 0:HB]
                        src = b[:, m * 4 * HB:(m + 1) * 4 * HB].rearrange("p (s n) -> p s n", s=4)
                        last = act.activation(dst, src, ACT.Copy)
                    last.then_inc(act_aux, 1)
                elif name == "new":
                    t, half = j // 2, j % 2
                    n = OUT_ROWS[t]
                    if t < 2 and half == 0:
                        wait_aux_read(act, aux("ca"))
                    if t >= 2 and half == 0:
                        act.wait_ge(stage_out[t % 2], 16 * (t // 2))
                    act.activation(stage[0:n, t % 2, half * 512:(half + 1) * 512], b[0:n, :], ACT.Copy)\
                       .then_inc(act_aux, 1)
                    if half == 1:
                        wait_aux_read(act, a)
                        act.dma_start(OUT_DST[t], stage[0:n, t % 2, :]).then_inc(stage_out[t % 2], 16)
                elif name == "x2T":
                    act.activation(xT[:, j, :], b[:, 0:N], ACT.Copy).then_inc(act_aux, 1)

            for a in range(aux("ca")):
                read_aux(a)
            act.wait_ge(weights_in[1], 16)
            act.dma_start(stage[0:NS * HA, 1, :], cache_a.rearrange("l s h d -> (l s h) d")).then_inc(cache_in, 16)
            act.dma_start(cvb[0:NS // 2 * HB, :, :].rearrange("p k n -> p (k n)")[:, 0:2 * D].rearrange(
                "p (t d) -> p t d", t=2), cache_b.rearrange("l (t s) h d -> (l s h) t d", t=2))\
                .then_inc(cache_in, 16)

            for g, (s, m, q) in enumerate(GROUPS):
                if g == group("GB", 4):
                    for a in range(aux("ca"), aux("new", 0)):
                        read_aux(a)
                if s in BY_ACT:
                    act.wait_ge(grp_done, g + 1)
                    b = bank[g % NBANK][:, 0:N]
                    if s == "GB":
                        if m >= 4:
                            wait_group_read(act, group("GA", m - 4))
                        act.activation(tmp[:, m % 4, :], b, ACT.Sigmoid).then_inc(act_grp, 1)
                    elif s == "C":
                        wait_group_read(act, group("GA", m + 4) if m < 4 else group("H", m - 4))
                        act.activation(tmp[:, m % 4, :], b, ACT.Copy).then_inc(act_grp, 1)
                    elif s == "Wa":
                        if m == 0:
                            act.wait_ge(aux_done, aux("mean"))
                            for h in range(2):
                                act.wait_ge(y_stored[h], 16)
                        act.activation(merged[:, m, :], b, ACT.Copy).then_inc(act_grp, 1)
                    elif s == "gA":
                        if m < 4:
                            wait_group_read(act, group("H", m + 4))
                        else:
                            act.wait_ge(gate_a_merged, m - 3)
                        act.activation(tmp[:, m % 4, :], b, ACT.Sigmoid, bias=vec[:, m, V_GATE:V_GATE + 1])\
                           .then_inc(act_grp, 1)
                    else:
                        act.activation(cva[:, m, :], b, ACT.Sigmoid, bias=vec[:, m, V_GATE + 1:V_GATE + 2])\
                           .then_inc(act_grp, 1)
                if g == group("B", 3):
                    for a in range(aux("new", 0), aux("mean")):
                        read_aux(a)
                if g == group("gB", 3):
                    for k in range(KB):
                        act.wait_ge(centred, k + 1)
                        act.activation(sq[:, k, :], cvb[:, k, :], ACT.Square).then_inc(squared, 1)
            act.wait_ge(conv_b_ops, 2 * KB * KB_TAPS)
            act.wait_ge(act_aux, ACT_AUX_NEW)
            act.dma_start(g2, norm2_g.to_broadcast([P, D])).then_inc(g_in, 16)
            act.dma_start(gf, final_g.rearrange("(a d) -> a d", a=1).to_broadcast([P, D])).then_inc(g_in, 16)
            act.dma_start(rw[:, :, 0:NG], group_w.rearrange("l (k p) g -> p (l k) g", p=P)).then_inc(rw_in, 16)
            act.dma_start(rw[:, :, NG:R], expert_w.rearrange("l (k p) g -> p (l k) g", p=P)).then_inc(rw_in, 16)
            act.dma_start(rbias[:, 0:NG], group_b.to_broadcast([P, NG])).then_inc(rw_in, 16)
            act.dma_start(rbias[:, NG:R], expert_b.to_broadcast([P, NE])).then_inc(rw_in, 16)
            act.wait_ge(root_in, 2)
            act.activation(sq[:, 0, :], sq[:, 1, :], ACT.Sqrt).then_inc(root_out, 1)
            for k in range(KB):
                act.wait_ge(scaled, k + 1)
                act.activation(cvb[:, k, :], cvb[:, k, :], ACT.Silu, scale=vec[:, k, V_LNG:V_LNG + 1],
                               bias=vec[:, k, V_LNB:V_LNB + 1]).then_inc(v_ready, 1)
            for i in range(NT):
                wait_group_read(act, WO_LAST[i])
                if i:
                    act.wait_ge(ssq_ready, NT + i)
                act.activation(junk, x_tok[:, i, :], ACT.Square, accum_out=small[:, i:i + 1]).then_inc(ssq_ready, 1)
            act.wait_ge(root_in, 3)
            act.activation(small[:, 8:8 + NT], small[:, 4:4 + NT], ACT.Sqrt).then_inc(root_out, 1)
            for a in range(aux("x2T", 0), aux("logit")):
                read_aux(a)
            for i in range(NT):
                act.wait_ge(aux_done, aux("x2T", KB - 1) + 1)
                act.activation(parts[0][:, i, :], n_tok[:, i, :], ACT.Copy).then_inc(part_ready[0], 1)
            act.wait_ge(exp_in, 1)
            act.activation(gexp, gexp, ACT.Exp).then_inc(exp_out, 1)
            act.activation(dexp, dexp, ACT.Exp).then_inc(exp_out, 1)
            for i in range(NT):
                act.wait_ge(rest_ready, i + 1)
                act.activation(parts[1][:, i, :], n_tok[:, i, :], ACT.Copy).then_inc(part_ready[1], 1)

            act.wait_ge(tables_ready, 1)
            items = act.value_load(table[0:1, 2 * NE:2 * NE + 1], min_val=NE, max_val=MAX_ITEMS)
            xe_f = xe.rearrange("p k t -> p (k t)")
            act.wait_ge(gathered, 1)
            act.activation(xe_f, XE, ACT.Copy).then_inc(xe_ready, 1)
            with act.Fori(0, items) as i:
                act.wait_ge(gate_up_done, i + 1)
                act.activation(sig, G, ACT.Silu).then_inc(sig_ready, 1)
                act.wait_ge(hid_turned, i + 1)
                act.activation(hidT.rearrange("p k t -> p (k t)"), HT, ACT.Copy).then_inc(hidT_ready, 1)
                act.wait_ge(gathered, i + 2)
                act.activation(xe_f, XE, ACT.Copy).then_inc(xe_ready, 1)

            for i in range(NT):
                act.wait_ge(final_ready, i + 1)
                if i:
                    act.wait_ge(ssq_ready, 2 * NT + i)
                act.activation(junk, x_tok[:, i, :], ACT.Square, accum_out=small[:, 16 + i:17 + i]).then_inc(ssq_ready, 1)
            act.wait_ge(root_in, 4)
            act.activation(small[:, 24:24 + NT], small[:, 20:20 + NT], ACT.Sqrt).then_inc(root_out, 1)
            for i in range(NT):
                act.wait_ge(normed, 2 * NT + i + 1)
                dst = y_prompt[0, i * P:(i + 1) * P, :] if i < NP // P else y_sample.rearrange("s t d -> (s t) d")
                act.dma_start(dst, n_tok[:, i, :]).then_inc(y_out, 16)
            act.wait_ge(y_out, 16 * NT)
            act.wait_ge(stage_out[0], 48)
            act.wait_ge(stage_out[1], 32)

        @block.vector
        def _(dve):
            chain = [0]

            def link(ins):
                chain[0] += 1
                ins.then_inc(dve_chain, 1)
                dve.wait_ge(dve_chain, chain[0])

            def rms_scale(n_ssq, n_root, src, mid, root, inv):
                dve.wait_ge(ssq_ready, n_ssq)
                dve.tensor_scalar(mid, src, 1.0 / D, 1e-6, ALU.mult, ALU.add).then_inc(root_in, 1)
                dve.wait_ge(root_out, n_root)
                link(dve.reciprocal(inv, root))

            rms_scale(NT, 1, small[:, 0:NT], small[:, 4:4 + NT], small[:, 8:8 + NT], small[:, 12:12 + NT])
            for i in range(NT):
                dve.tensor_scalar(n_tok[:, i, :], x_tok[:, i, :], small[:, 12 + i:13 + i], None, ALU.mult)\
                   .then_inc(normed, 1)

            def read_aux(a):
                name, j, eng = AUX[a]
                if eng != "dve":
                    return
                b = bank[4 + a % 4]
                dve.wait_ge(aux_done, a + 1)
                if name == "vec":
                    dve.tensor_copy(vec[:, :, :].rearrange("p k v -> p (k v)"), b[:, 0:KB * NV]).then_inc(dve_aux, 1)
                elif name == "xT":
                    dve.wait_ge(dve_aux, 1)
                    dve.tensor_scalar(xT[:, j, :], b[:, 0:N], vec[:, j, V_N1:V_N1 + 1], None, ALU.mult)\
                       .then_inc(dve_aux, 1)
                elif name == "ca":
                    for m in range(KB):
                        dst = ua_k[:, m, PA:WA].rearrange("p (s n) -> p s n", s=NS)[:, :, 0:HA]
                        src = b[:, m * NS * HA:(m + 1) * NS * HA].rearrange("p (s n) -> p s n", s=NS)
                        last = dve.tensor_copy(dst, src)
                    last.then_inc(dve_aux, 1)
                elif name == "x2T":
                    dve.tensor_copy(xT[:, j, :], b[:, 0:N]).then_inc(dve_aux, 1)

            for a in range(aux("ca")):
                read_aux(a)

            conv_b_at = {}
            ops = [0]

            def conv_b(half, tap):
                for m in range(4 * half, 4 * half + 4):
                    w = vec[:, m, V_CB + tap:V_CB + tap + 1]
                    for part, (src, dst) in enumerate(zip(ub_new(m, tap), both(cvb[:, m, :]))):
                        if tap == 0:
                            ins = dve.tensor_scalar(dst, src, w, vec[:, m, V_CBB:V_CBB + 1], ALU.mult, ALU.add)
                        else:
                            dve.wait_ge(conv_b_ops, conv_b_at[m, part])
                            ins = dve.scalar_tensor_tensor(dst, src, w, dst, ALU.mult, ALU.add)
                        ins.then_inc(conv_b_ops, 1)
                        ops[0] += 1
                        conv_b_at[m, part] = ops[0]

            a_ops = [0]

            def conv_a(m):
                for tap in range(KA_TAPS):
                    w = vec[:, m, V_CA + tap:V_CA + tap + 1]
                    for part, (src, dst) in enumerate(zip(ua_new(m, tap), both(cva[:, m, :]))):
                        if tap == 0:
                            ins = dve.tensor_scalar(dst, src, w, None, ALU.mult)
                        else:
                            dve.wait_ge(conv_a_ops, a_ops[0] - 1)
                            ins = dve.scalar_tensor_tensor(dst, src, w, dst, ALU.mult, ALU.add)
                        ins.then_inc(conv_a_ops, 1)
                        a_ops[0] += 1

            taps = [(0, k) for k in range(KB_TAPS)] + [(1, k) for k in range(KB_TAPS)]
            for g, (s, m, q) in enumerate(GROUPS):
                if s not in BY_ACT:
                    dve.wait_ge(grp_done, g + 1)
                    b = bank[g % NBANK]
                    if s == "GA":
                        wait_group_read(dve, group("GB", m))
                        for src, t, dst in zip(both(b[:, 0:N]), both(tmp[:, m % 4, :]), ub_new(m, HB)):
                            last = dve.tensor_tensor(dst, src, t, ALU.mult)
                        last.then_inc(dve_grp, 1)
                    elif s == "H":
                        wait_group_read(dve, group("C", m))
                        for src, t, dst in zip(both(b[:, 0:N]), both(tmp[:, m % 4, :]), ua_new(m, HA)):
                            last = dve.tensor_tensor(dst, src, t, ALU.mult)
                        last.then_inc(dve_grp, 1)
                        wait_group_read(dve, g)
                        conv_a(m)
                    elif s == "B":
                        dve.wait_ge(conv_a_ops, 2 * KA_TAPS * (m + 1))
                        dve.tensor_tensor(cva[:, m, :], b[:, 0:N], cva[:, m, :], ALU.mult).then_inc(dve_grp, 1)
                    elif s == "Wb":
                        wait_group_read(dve, group("gB", m))
                        dve.scalar_tensor_tensor(cva[:, m, :], b[:, 0:N], vec[:, m, V_BO:V_BO + 1], cva[:, m, :],
                                                 ALU.add, ALU.mult).then_inc(dve_grp, 1)
                    else:
                        half = q - (NCH - 2)
                        xs = x_tok[:, m, half * 512:(half + 1) * 512]
                        dve.tensor_tensor(xs, b[:, :], xs, ALU.add).then_inc(dve_grp, 1)
                if g == group("GA", 3):
                    wait_group_read(dve, g)
                    read_aux(aux("ca"))
                    dve.wait_ge(hist_zero, 2)
                    for j in range(4):
                        wait_aux_read(dve, aux("cb", j))
                    wait_aux_read(dve, aux("ca"))
                if g == group("GA", 7):
                    wait_group_read(dve, g)
                if g >= group("GB", 4) and taps:
                    for _ in range(2):
                        if taps and (taps[0][0] == 0 or g >= group("GA", 7)):
                            conv_b(*taps.pop(0))
                if g == group("Wa", KB - 1):
                    assert not taps
                    a = aux("mean")
                    dve.wait_ge(aux_done, a + 1)
                    for k in range(KB):
                        last = dve.scalar_tensor_tensor(cvb[:, k, :], bank[4 + a % 4][:, 0:N], -1.0 / D, cvb[:, k, :],
                                                        ALU.mult, ALU.add)
                        last.then_inc(centred, 1)
                    dve.wait_ge(centred, KB)
                    dve.tensor_copy(small[:, 40:41], small[:, 12:13]).then_inc(dve_aux, 1)
                if g == group("gB", KB - 1):
                    a = aux("var")
                    dve.wait_ge(aux_done, a + 1)
                    dve.tensor_scalar(sq[:, 1, :], bank[4 + a % 4][:, 0:N], 1.0 / D, 1e-5, ALU.mult, ALU.add).then_inc(dve_aux, 1)
                    wait_aux_read(dve, a)
                    dve.tensor_copy(small[:, 41:42], small[:, 12:13]).then_inc(root_in, 1)
                    dve.wait_ge(root_out, 2)
                    link(dve.reciprocal(sq[:, 2, :], sq[:, 0, :]))
                    for k in range(KB):
                        dve.tensor_tensor(cvb[:, k, :], cvb[:, k, :], sq[:, 2, :], ALU.mult).then_inc(scaled, 1)

            rms_scale(2 * NT, 3, small[:, 0:NT], small[:, 4:4 + NT], small[:, 8:8 + NT], small[:, 12:12 + NT])
            dve.wait_ge(g_in, 32)
            for i in range(NT):
                dve.scalar_tensor_tensor(n_tok[:, i, :], x_tok[:, i, :], small[:, 12 + i:13 + i], g2,
                                         ALU.mult, ALU.mult).then_inc(normed, 1)
            for a in range(aux("x2T", 0), aux("logit")):
                read_aux(a)

            dve.wait_ge(rw_in, 64)
            a = aux("logit")
            dve.wait_ge(aux_done, a + 1)
            link(dve.tensor_tensor(lg, bank[4 + a % 4][:, 0:NT * R].rearrange("p (i r) -> p i r", i=NT),
                                   rbias.unsqueeze(1).to_broadcast([P, NT, R]), ALU.add))
            dve.tensor_copy(small[:, 42:43], small[:, 12:13]).then_inc(dve_aux, 1)

            def spread(col, n):
                return col.unsqueeze(2).to_broadcast([P, NT, n])

            def first_max(values, n, best, hot_out, ta):
                link(dve.tensor_reduce(best, values, AX.X, ALU.max))
                link(dve.tensor_tensor(ta, values, spread(best, n), ALU.is_equal))
                link(dve.tensor_tensor(ta, ta, down_rank[:, 0:n].unsqueeze(1).to_broadcast([P, NT, n]), ALU.mult))
                link(dve.tensor_reduce(psum_g, ta, AX.X, ALU.max))
                link(dve.tensor_tensor(hot_out, ta, spread(psum_g, n), ALU.is_equal))

            dve.wait_ge(consts, 6)
            first_max(lg[:, :, 0:NG], NG, gmax, ghot, t0[:, :, 0:NG])
            link(dve.tensor_tensor(gexp, lg[:, :, 0:NG], spread(gmax, NG), ALU.subtract))
            gpen = t1[:, :, 0:NG]
            link(dve.tensor_scalar(gpen, ghot, BIG, -BIG, ALU.mult, ALU.add))
            for i in range(NT):
                gh = ghot[:, i, :].unsqueeze(2).to_broadcast([P, NG, EPG])
                gp = gpen[:, i, :].unsqueeze(2).to_broadcast([P, NG, EPG])
                lei = le[:, i, :].rearrange("p (g e) -> p g e", g=NG)
                link(dve.tensor_tensor(lei, lg[:, i, NG:R].rearrange("p (g e) -> p g e", g=NG), gh, ALU.mult))
                link(dve.tensor_tensor(lei, lei, gp, ALU.add))
            first_max(le, NE, top[0], hot[0], t0)
            link(dve.tensor_scalar(t1, hot[0], -BIG, None, ALU.mult))
            link(dve.tensor_tensor(le, le, t1, ALU.add))
            first_max(le, NE, top[1], hot[1], t0)
            dve.tensor_tensor(dexp, top[1], top[0], ALU.subtract).then_inc(exp_in, 1)
            dve.tensor_tensor(both_hot, hot[0], hot[1], ALU.add).then_inc(masks_ready, 1)

            dve.wait_ge(exp_out, 2)
            link(dve.tensor_reduce(psum_g, gexp, AX.X, ALU.add))
            link(dve.tensor_scalar(coef[1], dexp, 1.0, None, ALU.add))
            link(dve.tensor_tensor(coef[1], coef[1], psum_g, ALU.mult))
            link(dve.reciprocal(coef[0], coef[1]))
            link(dve.tensor_tensor(coef[1], dexp, coef[0], ALU.mult))

            a = aux("pos")
            b = bank[4 + a % 4]
            dve.wait_ge(aux_done, a + 1)
            link(dve.tensor_copy(cnt, b[0:NE, NT * NE:NT * NE + 1]))
            link(dve.tensor_scalar(ntile, cnt, float(T), 1.0, ALU.is_gt, ALU.add))
            for j in range(2, N // T):
                link(dve.scalar_tensor_tensor(ntile, cnt, float(j * T), ntile, ALU.is_gt, ALU.add))
            dve.tensor_scalar(ntile_b, ones[0:NE, :], ntile[:, 0:1], None, ALU.mult).then_inc(counts_ready, 1)
            link(dve.tensor_copy(t0, b[:, 0:NT * NE].rearrange("p (i e) -> p i e", i=NT)))
            dve.tensor_copy(small[:, 43:44], small[:, 12:13]).then_inc(dve_aux, 1)
            a = aux("table")
            b = bank[4 + a % 4]
            dve.wait_ge(aux_done, a + 1)
            link(dve.tensor_scalar(base_slot, b[:, 2 * NE + 1:3 * NE + 1], float(T), None, ALU.mult))
            dve.tensor_copy(table[:], b[0:1, 0:2 * NE + 1]).then_inc(tables_ready, 1)
            link(dve.tensor_tensor(t0, t0, base_slot.unsqueeze(1).to_broadcast([P, NT, NE]), ALU.add))
            for c in range(2):
                link(dve.tensor_tensor(t1, t0, hot[c], ALU.mult))
                link(dve.tensor_reduce(slot_f[c], t1, AX.X, ALU.add))
                link(dve.tensor_copy(slot_rem[:, c, :], slot_f[c]))
                link(dve.tensor_copy(slot_u32[c], slot_f[c]))
            dve.tensor_copy(small[:, 44:45], small[:, 12:13]).then_inc(slots_ready, 1)

            def pick_tokens():
                for i in range(NT):
                    dve.tensor_scalar(pick[:, i, :], iota[:, :], slot_rem[:, 0, i:i + 1], None, ALU.is_equal)\
                       .then_inc(pick_half, 1)
                for i in range(NT):
                    dve.wait_ge(pick_half, pick_base + i + 1)
                    last = dve.scalar_tensor_tensor(pick[:, i, :], iota[:, :], slot_rem[:, 1, i:i + 1],
                                                    pick[:, i, :], ALU.is_equal, ALU.add)
                last.then_inc(picked, 1)
                dve.wait_ge(picked, pick_n + 1)
                dve.tensor_scalar(slot_rem, slot_rem, -float(T), None, ALU.add).then_inc(rem_ready, 1)
                dve.wait_ge(rem_ready, pick_n + 1)

            dve.wait_ge(tables_ready, 1)
            dve.wait_ge(stage_out[0], 48)
            items = dve.value_load(table[0:1, 2 * NE:2 * NE + 1], min_val=NE, max_val=MAX_ITEMS)
            pick_base, pick_n = 0, 0
            pick_tokens()
            dve.wait_ge(gathered, 1)
            pick_base, pick_n = NT, 1
            pick_tokens()
            with dve.Fori(0, items) as i:
                dve.wait_ge(sig_ready, i + 1)
                dve.tensor_tensor(hid, U, sig, ALU.mult).then_inc(hid_ready, 1)
                dve.wait_ge(gathered, i + 2)
                pick_base, pick_n = NT * i + 2 * NT, i + 2
                pick_tokens()
                dve.wait_ge(down_done, i + 1)
                for h in range(2):
                    dve.wait_ge(y_stored[h], 16 * i + 16)
                dve.tensor_copy(y_half, Y[:, :]).then_inc(y_ready, 1)

            for h in range(2):
                dve.wait_ge(y_stored[h], 16 * items + 16)
            dve.tensor_copy(small[:, 45:46], small[:, 12:13]).then_inc(all_stored, 1)
            for i in range(NT):
                for c in range(2):
                    dve.wait_ge(rows_in[2 * i + c], 16)
                    rows = (rowsA if c == 0 else rowsB)[:, i, :]
                    ins = dve.scalar_tensor_tensor(x_tok[:, i, :], rows, coef[c][:, i:i + 1], x_tok[:, i, :],
                                                   ALU.mult, ALU.add)
                    if c == 0:
                        link(ins)
                    else:
                        ins.then_inc(final_ready, 1)
            rms_scale(3 * NT, 4, small[:, 16:16 + NT], small[:, 20:20 + NT], small[:, 24:24 + NT], small[:, 28:28 + NT])
            for i in range(NT):
                dve.scalar_tensor_tensor(n_tok[:, i, :], x_tok[:, i, :], small[:, 28 + i:29 + i], gf,
                                         ALU.mult, ALU.mult).then_inc(normed, 1)

        @block.tensor
        def _(pe):
            def start_aux(a):
                if a >= 4:
                    wait_aux_read(pe, a - 4)
                return bank[4 + a % 4]

            def end_aux(ins):
                ins.then_inc(aux_done, 1)

            pe.wait_ge(consts, 6)
            pe.wait_ge(vec_in, 16 * 8)
            b = start_aux(aux("vec"))
            for m in range(KB):
                last = pe.transpose(b[:, m * NV:(m + 1) * NV], stage[0:NV, 0, m * P:(m + 1) * P], ident[0:NV, 0:NV])
            end_aux(last)
            for k in range(KB):
                b = start_aux(aux("xT", k))
                for i in range(NT):
                    pe.wait_ge(normed, i + 1)
                    last = pe.transpose(b[:, i * P:(i + 1) * P], n_tok[:, i, k * P:(k + 1) * P], ident[:, :])
                end_aux(last)
            def cached_rows():
                pe.wait_ge(cache_in, 32)
                b = start_aux(aux("ca"))
                n = NS * HA
                for m in range(KB):
                    last = pe.transpose(b[:, m * n:(m + 1) * n], stage[0:n, 1, m * P:(m + 1) * P], ident[0:n, 0:n])
                end_aux(last)
                n = NS // 2 * HB
                cache_rows = cvb[:, :, :].rearrange("p k n -> p (k n)")[:, 0:2 * D].rearrange("p (t d) -> p t d", t=2)
                for j in range(4):
                    b = start_aux(aux("cb", j))
                    for m in range(4):
                        c0 = (4 * (j % 2) + m) * P
                        last = pe.transpose(b[:, m * n:(m + 1) * n], cache_rows[0:n, j // 2, c0:c0 + P], ident[0:n, 0:n])
                    end_aux(last)

            def new_rows(t, m):
                if t == 0:
                    return ua_k[:, m, PA - HA:PA]
                if t == 1:
                    return tails[:, m, 0:NS * HA]
                if t == 2:
                    return ub_k[:, m, PB - HB:PB]
                n = NS // 2 * HB
                return tails[:, m, NS * HA + (t - 3) * n:NS * HA + (t - 2) * n]

            for a in (aux("xT", KB - 1), aux("xT", KB - 2)):
                wait_aux_read(pe, a)
            for g, (s, m, q) in enumerate(GROUPS):
                if g == group("GB", 4):
                    cached_rows()
                slot, filled = slot_fill(q)
                pe.wait_ge(weights_in[slot], filled)
                if g >= NBANK:
                    wait_group_read(pe, g - NBANK)
                b = bank[g % NBANK]
                if s == "Wo":
                    pe.wait_ge(gate_b_merged, KB)
                    for k in range(KB):
                        last = pe.matmul(b[:, :], merged[:, k, m * P:(m + 1) * P], wide(slot)[:, k, :],
                                         start=(k == 0), stop=(k == KB - 1))
                else:
                    if s == "Wa" and m == 0:
                        wait_group_read(pe, group("B", KB - 1))
                    if s == "Wb" and m == 0:
                        pe.wait_ge(v_ready, KB)
                    src = {"Wa": cva, "Wb": cvb}.get(s, xT)
                    c0 = (m % 4) * P
                    for k in range(KB):
                        last = pe.matmul(b[:, 0:N], wide(slot)[:, k, c0:c0 + P], src[:, k, :],
                                         start=(k == 0), stop=(k == KB - 1))
                last.then_inc(grp_done, 1)
                if g == group("B", 3):
                    pe.wait_ge(tails_ready, 2 * KB)
                    for a in range(aux("new", 0), aux("mean")):
                        t, half = AUX[a][1] // 2, AUX[a][1] % 2
                        b = start_aux(a)
                        for m4 in range(4):
                            last = pe.transpose(b[0:OUT_ROWS[t], m4 * P:(m4 + 1) * P],
                                                new_rows(t, 4 * half + m4), ident[:, :])
                        end_aux(last)
                if g == group("Wa", KB - 1):
                    pe.wait_ge(conv_b_ops, 2 * KB * KB_TAPS)
                    b = start_aux(aux("mean"))
                    for k in range(KB):
                        last = pe.matmul(b[:, 0:N], ones[:, :], cvb[:, k, :], start=(k == 0), stop=(k == KB - 1))
                    end_aux(last)
                if g == group("gB", KB - 1):
                    pe.wait_ge(squared, KB)
                    b = start_aux(aux("var"))
                    for k in range(KB):
                        last = pe.matmul(b[:, 0:N], ones[:, :], sq[:, k, :], start=(k == 0), stop=(k == KB - 1))
                    end_aux(last)

            for k in range(KB):
                b = start_aux(aux("x2T", k))
                for i in range(NT):
                    pe.wait_ge(normed, NT + i + 1)
                    last = pe.transpose(b[:, i * P:(i + 1) * P], n_tok[:, i, k * P:(k + 1) * P], ident[:, :])
                end_aux(last)
            for a in (aux("x2T", KB - 1), aux("x2T", KB - 2)):
                wait_aux_read(pe, a)
            pe.wait_ge(rw_in, 64)
            b = start_aux(aux("logit"))
            for i in range(NT):
                for k in range(KB):
                    last = pe.matmul(b[:, i * R:(i + 1) * R], xT[:, k, i * P:(i + 1) * P], rw[:, k, :],
                                     start=(k == 0), stop=(k == KB - 1))
            end_aux(last)
            pe.wait_ge(masks_ready, 1)
            b = start_aux(aux("pos"))
            for i in range(NT):
                for j in range(i + 1):
                    pe.matmul(b[:, i * NE:(i + 1) * NE], before[:, :] if j == i else ones[:, :], both_hot[:, j, :],
                              start=(j == 0), stop=(j == i))
            for j in range(NT):
                last = pe.matmul(b[0:NE, NT * NE:NT * NE + 1], both_hot[:, j, :], ones[:, 0:1],
                                 start=(j == 0), stop=(j == NT - 1))
            end_aux(last)
            pe.wait_ge(counts_ready, 1)
            b = start_aux(aux("table"))
            pe.matmul(b[0:1, 0:NE], ntile, ident[0:NE, 0:NE], start=True, stop=True)
            pe.matmul(b[0:1, NE:2 * NE], ntile, before[0:NE, 0:NE], start=True, stop=True)
            pe.matmul(b[0:1, 2 * NE:2 * NE + 1], ntile, ones[0:NE, 0:1], start=True, stop=True)
            end_aux(pe.matmul(b[:, 2 * NE + 1:3 * NE + 1], ntile_b, before[0:NE, 0:NE], start=True, stop=True))

            def gather(blocks):
                for k in blocks:
                    for c in range(3):
                        for i in range(NT):
                            last = pe.matmul(XE[:, k * T:(k + 1) * T], parts[c][:, i, k * P:(k + 1) * P],
                                             pick[:, i, :], start=(c == 0 and i == 0), stop=(c == 2 and i == NT - 1))
                if KB - 1 in blocks:
                    last.then_inc(gathered, 1)

            pe.wait_ge(picked, 1)
            for part in part_ready:
                pe.wait_ge(part, NT)
            wait_group_read(pe, len(GROUPS) - 1)
            gather(range(KB))

            def item(i, slots, filled):
                pe.wait_ge(xe_ready, i + 1)
                pe.wait_ge(weights_in[slots[0]], filled[0])
                pe.wait_ge(weights_in[slots[1]], filled[1])
                for k in range(KB):
                    for dst, slot in ((G, slots[0]), (U, slots[1])):
                        last = pe.matmul(dst, xe[:, k, :], wide(slot)[:, k, :], start=(k == 0), stop=(k == KB - 1))
                last.then_inc(gate_up_done, 1)
                pe.wait_ge(picked, i + 2)
                gather(range(KB // 2 - 1))
                pe.wait_ge(hid_ready, i + 1)
                gather([KB // 2 - 1])
                for k in range(HK):
                    last = pe.transpose(HT[:, k * T:(k + 1) * T], hid[:, k * P:(k + 1) * P], ident[0:T, 0:T])
                last.then_inc(hid_turned, 1)
                gather(range(KB // 2, KB))
                pe.wait_ge(hidT_ready, i + 1)
                pe.wait_ge(weights_in[slots[2]], filled[2])
                for k in range(HK):
                    for h in range(2):
                        last = pe.matmul(Y[h * T:(h + 1) * T, :], hidT[:, k, :],
                                         deep(slots[2])[:, k, h * HALF:(h + 1) * HALF],
                                         start=(k == 0), stop=(k == HK - 1))
                last.then_inc(down_done, 1)

            pe.wait_ge(tables_ready, 1)
            with pe.Fori(0, NE // 2) as pair:
                for par in range(2):
                    e = pair * 2 + par
                    n = pe.value_load(table[0:1, bass.ds(e, 1)], min_val=1, max_val=N // T)
                    first = pe.value_load(table[0:1, bass.ds(e + NE, 1)], min_val=0, max_val=MAX_ITEMS - 1)
                    qs = [NCH + 3 * par + c for c in range(3)]
                    slots = [q % RING for q in qs]
                    filled = [pair * 16 + 16 * (q // RING + 1) for q in qs]
                    with pe.Fori(0, n) as j:
                        item(first + j, slots, filled)


_INS = ["x_prompt", "x_sample", "cache_conv_a", "cache_conv_b", "norm1_g", "w_in", "gate_b", "conv_a_w", "w_out_a",
        "conv_b_w", "conv_b_b", "ln_b_g", "ln_b_b", "w_out_b", "b_out_b", "w_o", "norm2_g", "router_group_w",
        "router_group_b", "router_expert_w", "router_expert_b", "exp_w_gate", "exp_w_up", "exp_w_down",
        "final_norm_g"]


def kernel(**inputs):
    import numpy as np
    import concourse.bacc as bacc
    from concourse.bass_utils import run_bass_kernel_spmd

    nc = bacc.Bacc("TRN2", target_bir_lowering=False, num_devices=1)
    arrays, args = {}, []
    for name in _INS:
        a = np.ascontiguousarray(inputs[name])
        arrays[f"in_{name}"] = a
        args.append(nc.dram_tensor(f"in_{name}", a.shape, mybir.dt.from_np(a.dtype), kind="ExternalInput").ap())
    xp, xs, ca, cb = (inputs[n].shape for n in _INS[:4])
    outs = [xp, xs, (ca[0], xp[0]) + tuple(ca[2:]), ca, (cb[0], xp[0]) + tuple(cb[2:]), cb]
    for i, shape in enumerate(outs):
        args.append(nc.dram_tensor(f"out_{i}", tuple(shape), F32, kind="ExternalOutput").ap())
    trunk_program(nc, *args)
    r = run_bass_kernel_spmd(nc, [arrays], core_ids=[0])
    return tuple(r.results[0][f"out_{i}"] for i in range(len(outs)))
```

```python
from contextlib import ExitStack

import concourse.bass as bass
from concourse import mybir

F32 = mybir.dt.float32
F32R = mybir.dt.float32r
I32 = mybir.dt.int32
U32 = mybir.dt.uint32
BF16 = mybir.dt.bfloat16
ALU = mybir.AluOpType
ACT = mybir.ActivationFunctionType
AX = mybir.AxisListType

P = 128


def trunk_program(nc, x_prompt, x_sample, cache_a, cache_b, norm1_g, w_in, gate_b, conv_a_w, w_out_a, conv_b_w,
                  conv_b_b, ln_b_g, ln_b_b, w_out_b, b_out_b, w_o, norm2_g, group_w, group_b, expert_w, expert_b,
                  w_gate, w_up, w_down, final_g, y_prompt, y_sample, new_a_prompt, new_a_sample, new_b_prompt,
                  new_b_sample):
    D = x_prompt.shape[2]
    NP = x_prompt.shape[1]
    NS, TS = x_sample.shape[0], x_sample.shape[1]
    N = NP + NS * TS
    NT = N // P
    KB = D // P
    KA_TAPS, KB_TAPS = conv_a_w.shape[1], conv_b_w.shape[1]
    HA, HB = KA_TAPS - 1, KB_TAPS - 1
    NE, DE = w_gate.shape[1], w_gate.shape[3]
    NG = group_w.shape[2]
    EPG = NE // NG
    HK = DE // P
    T = 64
    HALF = 512
    RING = 6
    MAX_ITEMS = NE + 2 * N // T
    R = NG + NE
    BIG = 1.0e30

    PA = HA + NP
    SA = HA + TS
    PB, SB = HB + NP, HB + TS
    WA, WB = PA + NS * SA, PB + NS * SB

    SECTION = {"B": 0, "C": 1, "H": 2, "GA": 3, "GB": 4, "gA": 5, "gB": 6}
    CHUNKS = [("GB", 0), ("GA", 0), ("GB", 1), ("GA", 1), ("C", 0), ("H", 0), ("C", 1), ("H", 1), ("B", 0),
              ("B", 1), ("Wa", 0), ("Wa", 1), ("gA", 0), ("gA", 1), ("gB", 0), ("gB", 1), ("Wb", 0), ("Wb", 1),
              ("Wo", 0), ("Wo", 1)]
    NCH = len(CHUNKS)
    GROUPS = []
    for q, (s, half) in enumerate(CHUNKS):
        for j in range(NT if s == "Wo" else HALF // P):
            GROUPS.append((s, j if s == "Wo" else half * (HALF // P) + j, q))
    UNITS = 2 * NCH
    UK = KB // 2
    NW = 3
    BY_ACT = ("GB", "C", "Wa", "gA", "gB")
    CHUNK_END = [1 + max(i for i, x in enumerate(GROUPS) if x[2] == q) for q in range(NCH)]
    NBANK = 4

    def group(s, m):
        return [i for i, x in enumerate(GROUPS) if x[0] == s and x[1] == m][0]

    AUX = [("vec", 0, "dve")]
    AUX += [("xT", k, "dve") for k in range(KB)]
    AUX += [("ca", 0, "dve")]
    AUX += [("cb", j, "act") for j in range(4)]
    OUT_TILES = ["ap", "as", "bp", "bs0", "bs1"]
    AUX += [("new", j, "act") for j in range(2 * len(OUT_TILES))]
    AUX += [("mean", 0, "dve"), ("var", 0, "dve")]
    AUX += [("x2T", k, "act" if k % 2 else "dve") for k in range(KB)]
    AUX += [("logit", 0, "dve"), ("pos", 0, "dve"), ("table", 0, "dve")]

    HEAD = 7
    PRODUCTS = {q: [] for q in range(NCH)}
    head = [("b", m, tap) for tap in range(1, HEAD) for m in range(KB // 2, KB)]
    for q, n in ((4, 8), (5, 8), (7, 8)):
        PRODUCTS[q] += [head.pop(0) for _ in range(n)]
    assert not head
    PRODUCTS[6] = [("a", m, tap) for m in range(KB // 2) for tap in range(1, KA_TAPS)]
    for q in (8, 9):
        PRODUCTS[q] = [("a", m, tap) for m in range(2 * q - 12, 2 * q - 10) for tap in range(1, KA_TAPS)]
    NPS = 4
    SLICES = {2: 4, 3: 5, 4: 4, 5: 5, 6: 4, 7: 5, 8: 4, 9: 5, 10: 5, 11: 5, 12: 5, 13: 4}
    MEAN_AT, VAR_AT, NEW_AT = 13, 14, 9

    def aux(name, j=0):
        return AUX.index([a for a in AUX if a[0] == name and a[1] == j][0])

    V_N1, V_GATE, V_CA, V_CB = 0, 1, 3, 3 + KA_TAPS
    V_CBB = V_CB + KB_TAPS
    V_LNG, V_LNB, V_BO = V_CBB + 1, V_CBB + 2, V_CBB + 3
    NV = V_BO + 1

    y_rows = nc.dram_tensor("expert_rows", (MAX_ITEMS * T, D), F32, kind="Internal").ap()

    with ExitStack() as ctx:
        def sb(name, shape, dt=F32):
            return ctx.enter_context(nc.sbuf_tensor(name, shape, dt))

        def sem(name):
            return ctx.enter_context(nc.semaphore(name))

        bank = [ctx.enter_context(nc.psum_tensor(f"bank{i}", [P, 512], F32)) for i in range(8)]
        arena_at = -(-nc.sbuf_base // 32) * 32
        arena = sb("arena", [P, RING * 4096])
        same_at = -(-nc.sbuf_base // 32) * 32
        same = sb("same", [P, 4 * KB * N])

        def at(name, shape, dt, offset):
            return nc.alloc_sbuf_tensor_at(name, shape, dt, offset=offset)

        UNIT = 4 * UK * HALF
        ACTS = 4 * KB * N
        ring = [at(f"ring{i}", [P, 4096], F32, arena_at + 2 * UNIT * i) for i in range(RING)]
        raw = [at(f"raw{i}", [P, UK, HALF], F32, arena_at + UNIT * i) for i in range(NW)]
        w_hi = [at(f"w_hi{i}", [P, UK, HALF], F32R, arena_at + UNIT * (NW + i)) for i in range(NW)]
        w_lo = [at(f"w_lo{i}", [P, UK, HALF], F32R, arena_at + UNIT * (2 * NW + i)) for i in range(NW)]
        x_lo = at("x_lo", [P, KB, N], F32R, arena_at + 3 * NW * UNIT)
        in_hi = at("in_hi", [P, KB, N], F32R, arena_at + 3 * NW * UNIT + ACTS)
        assert 3 * NW * UNIT + 2 * ACTS <= RING * 2 * UNIT
        x_hi = at("x_hi", [P, KB, N], F32R, same_at)
        x2T = at("x2T", [P, KB, N], F32, same_at)
        cva = at("cva", [P, KB, N], F32, same_at + ACTS)
        cva_lo = at("cva_lo", [P, KB, N], F32R, same_at + ACTS)
        cvb = at("cvb", [P, KB, N], F32, same_at + 2 * ACTS)
        cvb_lo = at("cvb_lo", [P, KB, N], F32R, same_at + 2 * ACTS)
        n_tok = at("n_tok", [P, NT, D], F32, same_at + 3 * ACTS)
        merged = at("merged", [P, KB, N], F32, same_at + 3 * ACTS)
        merged_lo = at("merged_lo", [P, KB, N], F32R, same_at + 3 * ACTS)
        x_tok = sb("x_tok", [P, NT, D])
        tails = n_tok[:, :, :].rearrange("p t d -> p (t d)")[:, 0:KB * NS * (HA + HB)].rearrange(
            "p (k n) -> p k n", k=KB)
        ua = sb("ua", [P, KB * WA])
        ub = sb("ub", [P, KB * WB])
        tmp = sb("tmp", [P, HALF // P, N])
        stage = sb("stage", [P, 2, D])
        product = stage[:, :, :].rearrange("p a d -> p (a d)")[:, 0:NPS * N].rearrange("p (s n) -> p s n", s=NPS)
        vec = sb("vec", [P, KB, NV])
        ident = sb("ident", [P, P])
        ones = sb("ones", [P, P])
        before = sb("before", [P, P])
        iota = sb("iota", [P, T])
        small = sb("small", [P, 48])
        rbias = sb("rbias", [P, R])[:, :]
        down_rank = sb("down_rank", [P, NE])[:, :]
        table = sb("table", [1, 2 * NE + 1], I32)

        ua_k = ua[:, :].rearrange("p (k n) -> p k n", k=KB)
        ub_k = ub[:, :].rearrange("p (k n) -> p k n", k=KB)

        def ua_new(m, tap):
            s = ua_k[:, m, PA:WA].rearrange("p (s n) -> p s n", s=NS)
            return ua_k[:, m, tap:tap + NP], s[:, :, tap:tap + TS]

        def ub_new(m, tap):
            s = ub_k[:, m, PB:WB].rearrange("p (s n) -> p s n", s=NS)
            return ub_k[:, m, tap:tap + NP], s[:, :, tap:tap + TS]

        def both(t):
            return t[:, 0:NP], t[:, NP:N].rearrange("p (s n) -> p s n", s=NS)

        sq = ua[:, 0:KB * N].rearrange("p (k n) -> p k n", k=KB)
        g2 = ub[:, 0:D]
        gf = ub[:, D:2 * D]
        junk = ub[:, 2 * D:3 * D]
        rw = ub[:, 3 * D:3 * D + KB * R].rearrange("p (k r) -> p k r", k=KB)
        ua_b, cva_b = ua[:, :].bitcast(BF16), cva[:, :, :].rearrange("p k n -> p (k n)").bitcast(BF16)
        parts = [x.rearrange("p (i d) -> p i d", d=D) for x in
                 (ua_b[:, 0:NT * D], ua_b[:, NT * D:2 * NT * D], cva_b[:, 0:NT * D])]
        pick = cvb[:, 0, 0:NT * T // 2].bitcast(BF16).rearrange("p (i t) -> p i t", i=NT)
        xe = cvb[:, 1:3, :].rearrange("p k n -> p (k n)")[:, 0:KB * T].rearrange("p (k t) -> p k t", k=KB)
        sig = cvb[:, 3:5, :].rearrange("p k n -> p (k n)")[T:2 * T, 0:DE]
        hid = cvb[:, 5:7, :].rearrange("p k n -> p (k n)")[0:T, 0:DE]
        hidT = cvb[:, 7, 0:HK * T].rearrange("p (k t) -> p k t", k=HK)
        y_half = stage[:, 0, 0:HALF]
        rowsA = x2T[:, :, :].rearrange("p k n -> p (k n)").rearrange("p (i d) -> p i d", d=D)
        rowsB = cva[:, :, :].rearrange("p k n -> p (k n)").rearrange("p (i d) -> p i d", d=D)
        rt = tmp[:, :, :].rearrange("p k n -> p (k n)")
        cols = [0]

        def scratch(n, rows=P):
            a = rt[0:rows, cols[0]:cols[0] + n]
            cols[0] += n
            return a

        x_in = sem("x_in")
        vec_in = sem("vec_in")
        cache_in = sem("cache_in")
        rw_in = sem("rw_in")
        g_in = sem("g_in")
        unit_in = [sem(f"unit_in{i}") for i in range(NW)]
        hi_ready = sem("hi_ready")
        lo_ready = sem("lo_ready")
        half_done = sem("half_done")
        x_hi_ready = sem("x_hi_ready")
        conv_first = sem("conv_first")
        product_ready = sem("product_ready")
        product_added = sem("product_added")
        in_hi_ready = sem("in_hi_ready")
        in_lo_ready = sem("in_lo_ready")
        v_done = sem("v_done")
        added = sem("added")
        merged_hi_ready = sem("merged_hi_ready")
        merged_lo_ready = sem("merged_lo_ready")
        weights_in = [sem(f"weights_in{i}") for i in range(RING)]
        consts = sem("consts")
        hist_zero = sem("hist_zero")
        ssq_ready = sem("ssq_ready")
        root_in = sem("root_in")
        root_out = sem("root_out")
        normed = sem("normed")
        grp_done = sem("grp_done")
        act_grp = sem("act_grp")
        dve_grp = sem("dve_grp")
        aux_done = sem("aux_done")
        act_aux = sem("act_aux")
        dve_aux = sem("dve_aux")
        conv_b_ops = sem("conv_b_ops")
        conv_a_ops = sem("conv_a_ops")
        dve_chain = sem("dve_chain")
        centred = sem("centred")
        squared = sem("squared")
        scaled = sem("scaled")
        gate_a_merged = sem("gate_a_merged")
        stage_out = [sem(f"stage_out{i}") for i in range(2)]
        tails_ready = sem("tails_ready")
        masks_ready = sem("masks_ready")
        exp_in = sem("exp_in")
        exp_out = sem("exp_out")
        counts_ready = sem("counts_ready")
        tables_ready = sem("tables_ready")
        picked = sem("picked")
        pick_half = sem("pick_half")
        rem_ready = sem("rem_ready")
        gathered = sem("gathered")
        xe_ready = sem("xe_ready")
        gate_up_done = sem("gate_up_done")
        hid_turned = sem("hid_turned")
        hidT_ready = sem("hidT_ready")
        part_ready = [sem(f"part{i}_ready") for i in range(3)]
        rest_ready = sem("rest_ready")
        blank_zero = sem("blank_zero")
        sig_ready = sem("sig_ready")
        hid_ready = sem("hid_ready")
        down_done = sem("down_done")
        y_ready = sem("y_ready")
        y_stored = [sem(f"y_stored{i}") for i in range(2)]
        slots_ready = sem("slots_ready")
        all_stored = sem("all_stored")
        rows_in = [sem(f"rows_in{i}") for i in range(2 * NT)]
        final_ready = sem("final_ready")
        y_out = sem("y_out")

        def wait_group_read(eng, g):
            by_act = GROUPS[g][0] in BY_ACT
            n = sum((x[0] in BY_ACT) == by_act for x in GROUPS[:g + 1])
            eng.wait_ge(act_grp if by_act else dve_grp, n)

        def wait_aux_read(eng, a):
            n = sum(x[2] == AUX[a][2] for x in AUX[:a + 1])
            eng.wait_ge(act_aux if AUX[a][2] == "act" else dve_aux, n)

        def wait_unit_used(eng, u):
            if u % 2:
                eng.wait_ge(grp_done, CHUNK_END[u // 2])
            else:
                eng.wait_ge(half_done, u // 2 + 1)

        def product_number(kind, m, tap):
            order = [x for q in range(NCH) for x in PRODUCTS[q]]
            return order.index((kind, m, tap)) + 1

        w_in_k = w_in.rearrange("l (k p) c -> p (l k) c", p=P)
        w_sq = {"Wa": w_out_a.rearrange("l (k p) c -> p (l k) c", p=P),
                "Wb": w_out_b.rearrange("l (k p) c -> p (l k) c", p=P),
                "Wo": w_o.rearrange("l (k p) c -> p (l k) c", p=P)}
        w_gu = {0: w_gate.rearrange("l e (k p) c -> (l e) p k c", p=P), 1: w_up.rearrange("l e (k p) c -> (l e) p k c", p=P)}
        w_dn = w_down.rearrange("l e (k p) c -> (l e) p k c", p=P)

        def wide(slot):
            return ring[slot][:, :].rearrange("p (k c) -> p k c", k=KB)

        def deep(slot):
            return ring[slot][:, :].rearrange("p (k c) -> p k c", k=HK)

        lg = scratch(NT * R).rearrange("p (i r) -> p i r", i=NT)
        gmax = scratch(NT)
        ghot = scratch(NT * NG).rearrange("p (i g) -> p i g", i=NT)
        gexp = scratch(NT * NG).rearrange("p (i g) -> p i g", i=NT)
        le = scratch(NT * NE).rearrange("p (i e) -> p i e", i=NT)
        hot = [scratch(NT * NE).rearrange("p (i e) -> p i e", i=NT) for _ in range(2)]
        t0 = scratch(NT * NE).rearrange("p (i e) -> p i e", i=NT)
        t1 = scratch(NT * NE).rearrange("p (i e) -> p i e", i=NT)
        both_hot = scratch(NT * NE).rearrange("p (i e) -> p i e", i=NT)
        top = [scratch(NT) for _ in range(2)]
        dexp = scratch(NT)
        coef = [scratch(NT) for _ in range(2)]
        psum_g = scratch(NT)
        slot_f = [scratch(NT) for _ in range(2)]
        slot_rem = scratch(2 * NT).rearrange("p (c i) -> p c i", c=2)
        slot_u32 = [scratch(NT).bitcast(U32) for _ in range(2)]
        cnt = scratch(1, NE)
        ntile = scratch(1, NE)
        ntile_b = scratch(P, NE)
        prefix = scratch(2 * NE + 1, NE)
        base_slot = scratch(NE)
        assert cols[0] <= 4 * N

        OUT_ROWS = [HA, NS * HA, HB, NS // 2 * HB, NS // 2 * HB]
        nbs = new_b_sample.rearrange("l s h d -> (l s h) d")
        OUT_DST = [new_a_prompt.rearrange("l b h d -> (l b h) d"), new_a_sample.rearrange("l s h d -> (l s h) d"),
                   new_b_prompt.rearrange("l b h d -> (l b h) d"), nbs[0:NS // 2 * HB, :], nbs[NS // 2 * HB:, :]]
        PRODUCT_COUNT = sum(len(x) for x in PRODUCTS.values())
        CONV_B_OPS = KB * (2 * KB_TAPS - HEAD)
        ACT_AUX_NEW = sum(x[2] == "act" for x in AUX[:aux("mean")])
        WO_LAST = [[i for i, x in enumerate(GROUPS) if x == ("Wo", t, NCH - 1)][0] for t in range(NT)]
        XE = bank[0][:, 0:KB * T]
        G, U = bank[1][0:T, :], bank[1][T:2 * T, :]
        HT = bank[2][:, 0:HK * T]
        Y = bank[3]

        block = ctx.enter_context(nc.Block())

        @block.sync
        def _(sp):
            sp.dma_start(x_tok[:, 0:NP // P, :], x_prompt[0].rearrange("(i p) d -> p i d", p=P)).then_inc(x_in, 16)
            sp.dma_start(x_tok[:, NP // P, :], x_sample.rearrange("s t d -> (s t) d")).then_inc(x_in, 16)
            sp.wait_ge(vec_in, 16 * 8)
            for u in range(UNITS):
                (s, half), k0 = CHUNKS[u // 2], u % 2 * UK
                if u >= NW:
                    sp.wait_ge(lo_ready, u - NW + 1)
                w, c0 = (w_sq[s], half * HALF) if s in w_sq else (w_in_k, SECTION[s] * D + half * HALF)
                sp.dma_start(raw[u % NW][:, :, :], w[:, k0:k0 + UK, c0:c0 + HALF]).then_inc(unit_in[u % NW], 16)

            def expert_weights(e, par, first):
                for c in range(3):
                    slot = 3 * par + c
                    if first:
                        sp.wait_ge(lo_ready, UNITS)
                        if slot:
                            sp.wait_ge(grp_done, len(GROUPS))
                    else:
                        sp.wait_ge([gate_up_done, gate_up_done, down_done][c], last_item)
                    dst, src = (deep(slot), w_dn) if c == 2 else (wide(slot), w_gu[c])
                    sp.dma_start(dst, src[e, :, :, :] if first else
                                 src[bass.ds(e, 1), :, :, :].rearrange("e p k c -> p (e k) c"))\
                      .then_inc(weights_in[slot], 16)

            expert_weights(0, 0, True)
            expert_weights(1, 1, True)
            sp.wait_ge(tables_ready, 1)
            with sp.Fori(1, NE // 2) as pair:
                for par in range(2):
                    last_item = sp.value_load(table[0:1, bass.ds(pair * 2 + (NE + par - 1), 1)], min_val=1, max_val=MAX_ITEMS)
                    expert_weights(pair * 2 + par, par, False)

        @block.gpsimd
        def _(pool):
            pool.memset(ident[:], 0.0).then_inc(consts, 1)
            pool.memset(ones[:], 1.0).then_inc(consts, 1)
            pool.wait_ge(consts, 2)
            pool.affine_select(out=ident[:], in_=ident[:], pattern=[[1, P]], compare_op=ALU.not_equal, fill=1.0,
                               base=0, channel_multiplier=-1).then_inc(consts, 1)
            pool.affine_select(out=before[:], in_=ones[:], pattern=[[1, P]], compare_op=ALU.is_gt, fill=0.0,
                               base=0, channel_multiplier=-1).then_inc(consts, 1)
            pool.iota(iota[:], pattern=[[1, T]], base=0, channel_multiplier=0,
                      allow_small_or_imprecise_dtypes=True).then_inc(consts, 1)
            pool.iota(down_rank, pattern=[[-1, NE]], base=NE, channel_multiplier=0,
                      allow_small_or_imprecise_dtypes=True).then_inc(consts, 1)
            pool.memset(ua_k[:, :, 0:HA], 0.0).then_inc(hist_zero, 1)
            pool.memset(ub_k[:, :, 0:HB], 0.0).then_inc(hist_zero, 1)
            def low_part(u):
                pool.wait_ge(hi_ready, u + 1)
                if u >= NW:
                    wait_unit_used(pool, u - NW)
                pool.tensor_tensor(w_lo[u % NW][:, :, :], raw[u % NW][:, :, :], w_hi[u % NW][:, :, :].bitcast(F32),
                                   ALU.subtract).then_inc(lo_ready, 1)

            low_part(0)
            low_part(1)
            for q, (s, half) in enumerate(CHUNKS):
                if 2 * q + 2 < UNITS:
                    low_part(2 * q + 2)
                todo = PRODUCTS[q]
                for n, (kind, m, tap) in enumerate(todo):
                    if n == len(todo) // 2:
                        low_part(2 * q + 3)
                    at_n = product_number(kind, m, tap)
                    pool.wait_ge(product_ready, at_n)
                    if tap > 1:
                        pool.wait_ge(product_added, product_number(kind, m, tap - 1))
                    cv = (cva if kind == "a" else cvb)[:, m, :]
                    pool.tensor_tensor(cv, cv, product[:, (at_n - 1) % NPS, :], ALU.add).then_inc(product_added, 1)
                if q == VAR_AT + 1:
                    for m in range(KB):
                        pool.wait_ge(in_hi_ready, KB + m + 1)
                        pool.tensor_tensor(cvb_lo[:, m, :], cvb[:, m, :], in_hi[:, m, :].bitcast(F32), ALU.subtract)\
                            .then_inc(in_lo_ready, 1)
                if 2 * q + 3 < UNITS and not todo:
                    low_part(2 * q + 3)
                if q == 1:
                    wait_aux_read(pool, aux("xT", KB - 1))
                    pool.memset(n_tok[:, NT - 1, :], 0.0).then_inc(blank_zero, 1)
                    pool.wait_ge(blank_zero, 1)
                    for h in range(2):
                        pool.dma_start(
                            y_rows[NE * T:MAX_ITEMS * T, h * HALF:(h + 1) * HALF].rearrange("(a p) d -> p a d", p=P),
                            n_tok[:, NT - 1, 0:HALF].unsqueeze(1).to_broadcast([P, (MAX_ITEMS - NE) * T // P, HALF]))\
                            .then_inc(y_stored[h], 16)
                for m in range(4 * half, 4 * half + 4):
                    if s == "B":
                        pool.wait_ge(in_hi_ready, m + 1)
                        pool.tensor_tensor(cva_lo[:, m, :], cva[:, m, :], in_hi[:, m, :].bitcast(F32), ALU.subtract)\
                            .then_inc(in_lo_ready, 1)
                    elif s == "gA":
                        wait_group_read(pool, group("gA", m))
                        pool.tensor_tensor(merged[:, m, :], merged[:, m, :], tmp[:, m % 4, :], ALU.mult)\
                            .then_inc(gate_a_merged, 1)
                    elif s == "Wb":
                        pool.wait_ge(merged_hi_ready, m + 1)
                        pool.tensor_tensor(merged_lo[:, m, :], merged[:, m, :], x_hi[:, m, :].bitcast(F32),
                                           ALU.subtract).then_inc(merged_lo_ready, 1)
            for i in range(NT):
                pool.wait_ge(part_ready[0], i + 1)
                pool.tensor_tensor(n_tok[:, i, :], n_tok[:, i, :], parts[0][:, i, :], ALU.subtract)\
                    .then_inc(rest_ready, 1)
            for i in range(NT):
                pool.wait_ge(part_ready[1], i + 1)
                pool.tensor_tensor(parts[2][:, i, :], n_tok[:, i, :], parts[1][:, i, :], ALU.subtract)\
                    .then_inc(part_ready[2], 1)
            pool.wait_ge(tables_ready, 1)
            for h in range(2):
                pool.wait_ge(y_stored[h], 16)
            items = pool.value_load(table[0:1, 2 * NE:2 * NE + 1], min_val=NE, max_val=MAX_ITEMS)
            with pool.Fori(0, items) as i:
                pool.wait_ge(y_ready, i + 1)
                for h in range(2):
                    pool.dma_start(y_rows[bass.ds(i * T, T), h * HALF:(h + 1) * HALF], y_half[h * T:(h + 1) * T, :])\
                        .then_inc(y_stored[h], 16)
            pool.wait_ge(slots_ready, 1)
            pool.wait_ge(all_stored, 1)
            for i in range(NT):
                for c in range(2):
                    pool.indirect_dma_start(
                        out=(rowsA if c == 0 else rowsB)[:, i, :], out_offset=None, in_=y_rows,
                        in_offset=bass.IndirectOffsetOnAxis(ap=slot_u32[c][:, i:i + 1], axis=0))\
                        .then_inc(rows_in[2 * i + c], 16)

        @block.scalar
        def _(act):
            rows = [(V_N1, norm1_g), (V_GATE, gate_b.rearrange("l (a d) -> (l a) d", d=D)),
                    (V_CA, conv_a_w.rearrange("l k d -> (l k) d")), (V_CB, conv_b_w.rearrange("l k d -> (l k) d")),
                    (V_CBB, conv_b_b), (V_LNG, ln_b_g), (V_LNB, ln_b_b), (V_BO, b_out_b)]
            for r, src in rows:
                act.dma_start(stage[r:r + src.shape[0], 0, :], src).then_inc(vec_in, 16)
            act.wait_ge(x_in, 32)
            for i in range(NT):
                act.activation(cva[:, :, :].rearrange("p k n -> p (k n)")[:, i * D:(i + 1) * D], x_tok[:, i, :],
                               ACT.Square, accum_out=small[:, i:i + 1]).then_inc(ssq_ready, 1)
            act.wait_ge(root_in, 1)
            act.activation(small[:, 8:8 + NT], small[:, 4:4 + NT], ACT.Sqrt).then_inc(root_out, 1)

            def read_aux(a):
                name, j, eng = AUX[a]
                if eng != "act":
                    return
                b = bank[4 + a % 4]
                act.wait_ge(aux_done, a + 1)
                if name == "cb":
                    t, mh = j // 2, j % 2
                    for m in range(4):
                        dst = ub_k[:, 4 * mh + m, PB:WB].rearrange("p (s n) -> p s n", s=NS)[
                            :, 4 * t:4 * t + 4, 0:HB]
                        src = b[:, m * 4 * HB:(m + 1) * 4 * HB].rearrange("p (s n) -> p s n", s=4)
                        last = act.activation(dst, src, ACT.Copy)
                    last.then_inc(act_aux, 1)
                elif name == "new":
                    t, half = j // 2, j % 2
                    n = OUT_ROWS[t]
                    if t < 2 and half == 0:
                        wait_aux_read(act, aux("ca"))
                    if t >= 2 and half == 0:
                        act.wait_ge(stage_out[t % 2], 16 * (t // 2))
                    act.activation(stage[0:n, t % 2, half * 512:(half + 1) * 512], b[0:n, :], ACT.Copy)\
                       .then_inc(act_aux, 1)
                    if half == 1:
                        wait_aux_read(act, a)
                        act.dma_start(OUT_DST[t], stage[0:n, t % 2, :]).then_inc(stage_out[t % 2], 16)
                elif name == "x2T":
                    act.activation(x2T[:, j, :], b[:, 0:N], ACT.Copy).then_inc(act_aux, 1)

            def high_part(u):
                act.wait_ge(unit_in[u % NW], 16 * (u // NW + 1))
                if u >= NW:
                    wait_unit_used(act, u - NW)
                act.activation(w_hi[u % NW][:, :, :], raw[u % NW][:, :, :], ACT.Copy).then_inc(hi_ready, 1)

            high_part(0)
            act.wait_ge(dve_aux, 1)
            for k in range(KB):
                a = aux("xT", k)
                act.wait_ge(aux_done, a + 1)
                act.activation(x_hi[:, k, :], bank[4 + a % 4][:, 0:N], ACT.Copy, scale=vec[:, k, V_N1:V_N1 + 1])\
                   .then_inc(x_hi_ready, 1)
            high_part(1)
            act.wait_ge(unit_in[1], 16)
            act.dma_start(stage[0:NS * HA, 1, :], cache_a.rearrange("l s h d -> (l s h) d")).then_inc(cache_in, 16)
            act.dma_start(cvb[0:NS // 2 * HB, :, :].rearrange("p k n -> p (k n)")[:, 0:2 * D].rearrange(
                "p (t d) -> p t d", t=2), cache_b.rearrange("l (t s) h d -> (l s h) t d", t=2))\
                .then_inc(cache_in, 16)

            def form_product(kind, m, tap):
                n = product_number(kind, m, tap)
                if n > NPS:
                    act.wait_ge(product_added, n - NPS)
                src, v = (ua_new, V_CA) if kind == "a" else (ub_new, V_CB)
                for x, y in zip(src(m, tap), both(product[:, (n - 1) % NPS, :])):
                    last = act.activation(y, x, ACT.Copy, scale=vec[:, m, v + tap:v + tap + 1])
                last.then_inc(product_ready, 1)

            def high_in(m, src):
                act.activation(in_hi[:, m, :], src, ACT.Copy).then_inc(in_hi_ready, 1)

            for q, (s, half) in enumerate(CHUNKS):
                if 2 * q + 2 < UNITS:
                    high_part(2 * q + 2)
                if q == 4:
                    wait_group_read(act, group("GA", KB - 1))
                    for m in range(KB // 2, KB):
                        for x, y in zip(ub_new(m, 0), both(cvb[:, m, :])):
                            last = act.activation(y, x, ACT.Identity, scale=vec[:, m, V_CB:V_CB + 1],
                                                  bias=vec[:, m, V_CBB:V_CBB + 1])
                        last.then_inc(conv_first, 1)
                if q in (6, 8):
                    for m in range(2 * q - 12, 2 * q - 8):
                        wait_group_read(act, group("H", m))
                        for x, y in zip(ua_new(m, 0), both(cva[:, m, :])):
                            last = act.activation(y, x, ACT.Copy, scale=vec[:, m, V_CA:V_CA + 1])
                        last.then_inc(conv_first, 1)
                todo = PRODUCTS[q]
                for n, x in enumerate(todo):
                    if n == len(todo) // 2:
                        high_part(2 * q + 3)
                    form_product(*x)
                if not todo and 2 * q + 3 < UNITS and q != VAR_AT + 1:
                    high_part(2 * q + 3)
                if q == NEW_AT:
                    wait_group_read(act, group("H", KB - 1))
                    for m in range(KB):
                        for src, first, last_col, h in ((ua_k[:, m, PA:WA], 0, SA, HA),
                                                        (ub_k[:, m, PB:WB], NS * HA, SB, HB)):
                            act.activation(
                                tails[:, m, first:first + NS * h].rearrange("p (s n) -> p s n", s=NS),
                                src.rearrange("p (s n) -> p s n", s=NS)[:, :, last_col - h:last_col],
                                ACT.Copy).then_inc(tails_ready, 1)
                if q == VAR_AT:
                    for k in range(KB):
                        act.wait_ge(centred, k + 1)
                        act.activation(sq[:, k, :], cvb[:, k, :], ACT.Square).then_inc(squared, 1)
                if q == VAR_AT + 1:
                    act.wait_ge(root_in, 2)
                    act.activation(sq[:, 0, :], sq[:, 1, :], ACT.Sqrt).then_inc(root_out, 1)
                    for k in range(KB):
                        act.wait_ge(scaled, k + 1)
                        act.activation(cvb[:, k, :], cvb[:, k, :], ACT.Silu, scale=vec[:, k, V_LNG:V_LNG + 1],
                                       bias=vec[:, k, V_LNB:V_LNB + 1]).then_inc(v_done, 1)
                        act.wait_ge(v_done, k + 1)
                        high_in(k, cvb[:, k, :])
                    high_part(2 * q + 3)
                for g in [i for i, x in enumerate(GROUPS) if x[2] == q]:
                    m = GROUPS[g][1]
                    b = bank[g % NBANK][:, 0:N]
                    if s in BY_ACT:
                        act.wait_ge(grp_done, g + 1)
                    if s == "GB":
                        if m >= 4:
                            wait_group_read(act, group("GA", m - 4))
                        act.activation(tmp[:, m % 4, :], b, ACT.Sigmoid).then_inc(act_grp, 1)
                    elif s == "C":
                        wait_group_read(act, group("GA", m + 4) if m < 4 else group("H", m - 4))
                        act.activation(tmp[:, m % 4, :], b, ACT.Copy).then_inc(act_grp, 1)
                    elif s == "Wa":
                        if m == 0:
                            act.wait_ge(aux_done, aux("mean"))
                            for h in range(2):
                                act.wait_ge(y_stored[h], 16)
                        act.activation(merged[:, m, :], b, ACT.Copy).then_inc(act_grp, 1)
                    elif s == "gA":
                        if m < 4:
                            wait_group_read(act, group("H", m + 4))
                        else:
                            act.wait_ge(gate_a_merged, m - 3)
                        act.activation(tmp[:, m % 4, :], b, ACT.Sigmoid, bias=vec[:, m, V_GATE:V_GATE + 1])\
                           .then_inc(act_grp, 1)
                    elif s == "gB":
                        act.activation(cva[:, m, :], b, ACT.Sigmoid, bias=vec[:, m, V_GATE + 1:V_GATE + 2])\
                           .then_inc(act_grp, 1)
                    elif s == "B":
                        wait_group_read(act, g)
                        high_in(m, cva[:, m, :])
                    elif s == "Wb":
                        act.wait_ge(added, m + 1)
                        act.activation(x_hi[:, m, :], merged[:, m, :], ACT.Copy).then_inc(merged_hi_ready, 1)
                if q == 1:
                    for a in range(aux("ca"), aux("new", 0)):
                        read_aux(a)
                if q == NEW_AT:
                    act.wait_ge(product_added, PRODUCT_COUNT)
                    for a in range(aux("new", 0), aux("mean")):
                        read_aux(a)
            act.wait_ge(conv_b_ops, CONV_B_OPS)
            act.wait_ge(act_aux, ACT_AUX_NEW)
            act.dma_start(g2, norm2_g.to_broadcast([P, D])).then_inc(g_in, 16)
            act.dma_start(gf, final_g.rearrange("(a d) -> a d", a=1).to_broadcast([P, D])).then_inc(g_in, 16)
            act.dma_start(rw[:, :, 0:NG], group_w.rearrange("l (k p) g -> p (l k) g", p=P)).then_inc(rw_in, 16)
            act.dma_start(rw[:, :, NG:R], expert_w.rearrange("l (k p) g -> p (l k) g", p=P)).then_inc(rw_in, 16)
            act.dma_start(rbias[:, 0:NG], group_b.to_broadcast([P, NG])).then_inc(rw_in, 16)
            act.dma_start(rbias[:, NG:R], expert_b.to_broadcast([P, NE])).then_inc(rw_in, 16)
            for i in range(NT):
                wait_group_read(act, WO_LAST[i])
                if i:
                    act.wait_ge(ssq_ready, NT + i)
                act.activation(junk, x_tok[:, i, :], ACT.Square, accum_out=small[:, i:i + 1]).then_inc(ssq_ready, 1)
            act.wait_ge(root_in, 3)
            act.activation(small[:, 8:8 + NT], small[:, 4:4 + NT], ACT.Sqrt).then_inc(root_out, 1)
            for a in range(aux("x2T", 0), aux("logit")):
                read_aux(a)
            for i in range(NT):
                act.wait_ge(aux_done, aux("x2T", KB - 1) + 1)
                act.activation(parts[0][:, i, :], n_tok[:, i, :], ACT.Copy).then_inc(part_ready[0], 1)
            act.wait_ge(exp_in, 1)
            act.activation(gexp, gexp, ACT.Exp).then_inc(exp_out, 1)
            act.activation(dexp, dexp, ACT.Exp).then_inc(exp_out, 1)
            for i in range(NT):
                act.wait_ge(rest_ready, i + 1)
                act.activation(parts[1][:, i, :], n_tok[:, i, :], ACT.Copy).then_inc(part_ready[1], 1)

            act.wait_ge(tables_ready, 1)
            items = act.value_load(table[0:1, 2 * NE:2 * NE + 1], min_val=NE, max_val=MAX_ITEMS)
            xe_f = xe.rearrange("p k t -> p (k t)")
            act.wait_ge(gathered, 1)
            act.activation(xe_f, XE, ACT.Copy).then_inc(xe_ready, 1)
            with act.Fori(0, items) as i:
                act.wait_ge(gate_up_done, i + 1)
                act.activation(sig, G, ACT.Silu).then_inc(sig_ready, 1)
                act.wait_ge(hid_turned, i + 1)
                act.activation(hidT.rearrange("p k t -> p (k t)"), HT, ACT.Copy).then_inc(hidT_ready, 1)
                act.wait_ge(gathered, i + 2)
                act.activation(xe_f, XE, ACT.Copy).then_inc(xe_ready, 1)

            for i in range(NT):
                act.wait_ge(final_ready, i + 1)
                if i:
                    act.wait_ge(ssq_ready, 2 * NT + i)
                act.activation(junk, x_tok[:, i, :], ACT.Square, accum_out=small[:, 16 + i:17 + i]).then_inc(ssq_ready, 1)
            act.wait_ge(root_in, 4)
            act.activation(small[:, 24:24 + NT], small[:, 20:20 + NT], ACT.Sqrt).then_inc(root_out, 1)
            for i in range(NT):
                act.wait_ge(normed, 2 * NT + i + 1)
                dst = y_prompt[0, i * P:(i + 1) * P, :] if i < NP // P else y_sample.rearrange("s t d -> (s t) d")
                act.dma_start(dst, n_tok[:, i, :]).then_inc(y_out, 16)
            act.wait_ge(y_out, 16 * NT)
            act.wait_ge(stage_out[0], 48)
            act.wait_ge(stage_out[1], 32)

        @block.vector
        def _(dve):
            chain = [0]

            def link(ins):
                chain[0] += 1
                ins.then_inc(dve_chain, 1)
                dve.wait_ge(dve_chain, chain[0])

            def rms_scale(n_ssq, n_root, src, mid, root, inv):
                dve.wait_ge(ssq_ready, n_ssq)
                dve.tensor_scalar(mid, src, 1.0 / D, 1e-6, ALU.mult, ALU.add).then_inc(root_in, 1)
                dve.wait_ge(root_out, n_root)
                link(dve.reciprocal(inv, root))

            rms_scale(NT, 1, small[:, 0:NT], small[:, 4:4 + NT], small[:, 8:8 + NT], small[:, 12:12 + NT])
            for i in range(NT):
                dve.tensor_scalar(n_tok[:, i, :], x_tok[:, i, :], small[:, 12 + i:13 + i], None, ALU.mult)\
                   .then_inc(normed, 1)

            def read_aux(a):
                name, j, eng = AUX[a]
                if eng != "dve":
                    return
                b = bank[4 + a % 4]
                dve.wait_ge(aux_done, a + 1)
                if name == "vec":
                    dve.tensor_copy(vec[:, :, :].rearrange("p k v -> p (k v)"), b[:, 0:KB * NV]).then_inc(dve_aux, 1)
                elif name == "xT":
                    dve.wait_ge(dve_aux, 1)
                    dve.wait_ge(x_hi_ready, j + 1)
                    dve.scalar_tensor_tensor(x_lo[:, j, :], b[:, 0:N], vec[:, j, V_N1:V_N1 + 1],
                                             x_hi[:, j, :].bitcast(F32), ALU.mult, ALU.subtract).then_inc(dve_aux, 1)
                elif name == "ca":
                    for m in range(KB):
                        dst = ua_k[:, m, PA:WA].rearrange("p (s n) -> p s n", s=NS)[:, :, 0:HA]
                        src = b[:, m * NS * HA:(m + 1) * NS * HA].rearrange("p (s n) -> p s n", s=NS)
                        last = dve.tensor_copy(dst, src)
                    last.then_inc(dve_aux, 1)
                elif name == "x2T":
                    dve.tensor_copy(x2T[:, j, :], b[:, 0:N]).then_inc(dve_aux, 1)

            for a in range(aux("ca")):
                read_aux(a)

            conv_b_at = {}
            ops = [0]

            def conv_b(half, tap):
                for m in range(4 * half, 4 * half + 4):
                    w = vec[:, m, V_CB + tap:V_CB + tap + 1]
                    if half == 1 and tap == HEAD:
                        dve.wait_ge(product_added, product_number("b", m, HEAD - 1))
                    for part, (src, dst) in enumerate(zip(ub_new(m, tap), both(cvb[:, m, :]))):
                        if tap == 0:
                            ins = dve.tensor_scalar(dst, src, w, vec[:, m, V_CBB:V_CBB + 1], ALU.mult, ALU.add)
                        else:
                            if (m, part) in conv_b_at:
                                dve.wait_ge(conv_b_ops, conv_b_at[m, part])
                            ins = dve.scalar_tensor_tensor(dst, src, w, dst, ALU.mult, ALU.add)
                        ins.then_inc(conv_b_ops, 1)
                        ops[0] += 1
                        conv_b_at[m, part] = ops[0]

            def read_group(g):
                s, m, q = GROUPS[g]
                dve.wait_ge(grp_done, g + 1)
                b = bank[g % NBANK]
                if s == "GA":
                    wait_group_read(dve, group("GB", m))
                    for src, t, dst in zip(both(b[:, 0:N]), both(tmp[:, m % 4, :]), ub_new(m, HB)):
                        last = dve.tensor_tensor(dst, src, t, ALU.mult)
                    last.then_inc(dve_grp, 1)
                elif s == "H":
                    wait_group_read(dve, group("C", m))
                    for src, t, dst in zip(both(b[:, 0:N]), both(tmp[:, m % 4, :]), ua_new(m, HA)):
                        last = dve.tensor_tensor(dst, src, t, ALU.mult)
                    last.then_inc(dve_grp, 1)
                elif s == "B":
                    dve.wait_ge(product_added, product_number("a", m, KA_TAPS - 1))
                    dve.tensor_tensor(cva[:, m, :], b[:, 0:N], cva[:, m, :], ALU.mult).then_inc(dve_grp, 1)
                elif s == "Wb":
                    wait_group_read(dve, group("gB", m))
                    dve.wait_ge(gate_a_merged, m + 1)
                    dve.scalar_tensor_tensor(cva[:, m, :], b[:, 0:N], vec[:, m, V_BO:V_BO + 1], cva[:, m, :],
                                             ALU.add, ALU.mult).then_inc(dve_grp, 1)
                    wait_group_read(dve, g)
                    dve.tensor_tensor(merged[:, m, :], merged[:, m, :], cva[:, m, :], ALU.add).then_inc(added, 1)
                else:
                    half = q - (NCH - 2)
                    xs = x_tok[:, m, half * 512:(half + 1) * 512]
                    dve.tensor_tensor(xs, b[:, :], xs, ALU.add).then_inc(dve_grp, 1)

            taps = [(0, k) for k in range(KB_TAPS)] + [(1, k) for k in range(HEAD, KB_TAPS)]
            for q, (s, half) in enumerate(CHUNKS):
                groups = [i for i, x in enumerate(GROUPS) if x[2] == q]
                n_slices = SLICES.get(q, 0)
                for _ in range(min(2, n_slices)):
                    conv_b(*taps.pop(0))
                for j, g in enumerate(groups):
                    if s not in BY_ACT:
                        read_group(g)
                    if 2 + j < n_slices:
                        conv_b(*taps.pop(0))
                if q in (1, 3):
                    wait_group_read(dve, groups[-1])
                if q == 1:
                    read_aux(aux("ca"))
                    dve.wait_ge(hist_zero, 2)
                    for j in range(4):
                        wait_aux_read(dve, aux("cb", j))
                    wait_aux_read(dve, aux("ca"))
                if q == MEAN_AT:
                    assert not taps
                    a = aux("mean")
                    dve.wait_ge(aux_done, a + 1)
                    for k in range(KB):
                        last = dve.scalar_tensor_tensor(cvb[:, k, :], bank[4 + a % 4][:, 0:N], -1.0 / D, cvb[:, k, :],
                                                        ALU.mult, ALU.add)
                        last.then_inc(centred, 1)
                    dve.wait_ge(centred, KB)
                    dve.tensor_copy(small[:, 40:41], small[:, 12:13]).then_inc(dve_aux, 1)
                if q == VAR_AT:
                    a = aux("var")
                    dve.wait_ge(aux_done, a + 1)
                    dve.tensor_scalar(sq[:, 1, :], bank[4 + a % 4][:, 0:N], 1.0 / D, 1e-5, ALU.mult, ALU.add)\
                       .then_inc(dve_aux, 1)
                    wait_aux_read(dve, a)
                    dve.tensor_copy(small[:, 41:42], small[:, 12:13]).then_inc(root_in, 1)
                    dve.wait_ge(root_out, 2)
                    link(dve.reciprocal(sq[:, 2, :], sq[:, 0, :]))
                    for k in range(KB):
                        dve.tensor_tensor(cvb[:, k, :], cvb[:, k, :], sq[:, 2, :], ALU.mult).then_inc(scaled, 1)

            rms_scale(2 * NT, 3, small[:, 0:NT], small[:, 4:4 + NT], small[:, 8:8 + NT], small[:, 12:12 + NT])
            dve.wait_ge(g_in, 32)
            for i in range(NT):
                dve.scalar_tensor_tensor(n_tok[:, i, :], x_tok[:, i, :], small[:, 12 + i:13 + i], g2,
                                         ALU.mult, ALU.mult).then_inc(normed, 1)
            for a in range(aux("x2T", 0), aux("logit")):
                read_aux(a)

            dve.wait_ge(rw_in, 64)
            a = aux("logit")
            dve.wait_ge(aux_done, a + 1)
            link(dve.tensor_tensor(lg, bank[4 + a % 4][:, 0:NT * R].rearrange("p (i r) -> p i r", i=NT),
                                   rbias.unsqueeze(1).to_broadcast([P, NT, R]), ALU.add))
            dve.tensor_copy(small[:, 42:43], small[:, 12:13]).then_inc(dve_aux, 1)

            def spread(col, n):
                return col.unsqueeze(2).to_broadcast([P, NT, n])

            def first_max(values, n, best, hot_out, ta):
                link(dve.tensor_reduce(best, values, AX.X, ALU.max))
                link(dve.tensor_tensor(ta, values, spread(best, n), ALU.is_equal))
                link(dve.tensor_tensor(ta, ta, down_rank[:, 0:n].unsqueeze(1).to_broadcast([P, NT, n]), ALU.mult))
                link(dve.tensor_reduce(psum_g, ta, AX.X, ALU.max))
                link(dve.tensor_tensor(hot_out, ta, spread(psum_g, n), ALU.is_equal))

            dve.wait_ge(consts, 6)
            first_max(lg[:, :, 0:NG], NG, gmax, ghot, t0[:, :, 0:NG])
            link(dve.tensor_tensor(gexp, lg[:, :, 0:NG], spread(gmax, NG), ALU.subtract))
            gpen = t1[:, :, 0:NG]
            link(dve.tensor_scalar(gpen, ghot, BIG, -BIG, ALU.mult, ALU.add))
            for i in range(NT):
                gh = ghot[:, i, :].unsqueeze(2).to_broadcast([P, NG, EPG])
                gp = gpen[:, i, :].unsqueeze(2).to_broadcast([P, NG, EPG])
                lei = le[:, i, :].rearrange("p (g e) -> p g e", g=NG)
                link(dve.tensor_tensor(lei, lg[:, i, NG:R].rearrange("p (g e) -> p g e", g=NG), gh, ALU.mult))
                link(dve.tensor_tensor(lei, lei, gp, ALU.add))
            first_max(le, NE, top[0], hot[0], t0)
            link(dve.tensor_scalar(t1, hot[0], -BIG, None, ALU.mult))
            link(dve.tensor_tensor(le, le, t1, ALU.add))
            first_max(le, NE, top[1], hot[1], t0)
            dve.tensor_tensor(dexp, top[1], top[0], ALU.subtract).then_inc(exp_in, 1)
            dve.tensor_tensor(both_hot, hot[0], hot[1], ALU.add).then_inc(masks_ready, 1)

            dve.wait_ge(exp_out, 2)
            link(dve.tensor_reduce(psum_g, gexp, AX.X, ALU.add))
            link(dve.tensor_scalar(coef[1], dexp, 1.0, None, ALU.add))
            link(dve.tensor_tensor(coef[1], coef[1], psum_g, ALU.mult))
            link(dve.reciprocal(coef[0], coef[1]))
            link(dve.tensor_tensor(coef[1], dexp, coef[0], ALU.mult))

            a = aux("pos")
            b = bank[4 + a % 4]
            dve.wait_ge(aux_done, a + 1)
            link(dve.tensor_copy(cnt, b[0:NE, NT * NE:NT * NE + 1]))
            link(dve.tensor_scalar(ntile, cnt, float(T), 1.0, ALU.is_gt, ALU.add))
            for j in range(2, N // T):
                link(dve.scalar_tensor_tensor(ntile, cnt, float(j * T), ntile, ALU.is_gt, ALU.add))
            dve.tensor_scalar(ntile_b, ones[0:NE, :], ntile[:, 0:1], None, ALU.mult).then_inc(counts_ready, 1)
            link(dve.tensor_copy(t0, b[:, 0:NT * NE].rearrange("p (i e) -> p i e", i=NT)))
            dve.tensor_copy(small[:, 43:44], small[:, 12:13]).then_inc(dve_aux, 1)
            a = aux("table")
            b = bank[4 + a % 4]
            dve.wait_ge(aux_done, a + 1)
            link(dve.tensor_scalar(base_slot, b[:, 2 * NE + 1:3 * NE + 1], float(T), None, ALU.mult))
            dve.tensor_copy(table[:], b[0:1, 0:2 * NE + 1]).then_inc(tables_ready, 1)
            link(dve.tensor_tensor(t0, t0, base_slot.unsqueeze(1).to_broadcast([P, NT, NE]), ALU.add))
            for c in range(2):
                link(dve.tensor_tensor(t1, t0, hot[c], ALU.mult))
                link(dve.tensor_reduce(slot_f[c], t1, AX.X, ALU.add))
                link(dve.tensor_copy(slot_rem[:, c, :], slot_f[c]))
                link(dve.tensor_copy(slot_u32[c], slot_f[c]))
            dve.tensor_copy(small[:, 44:45], small[:, 12:13]).then_inc(slots_ready, 1)

            def pick_tokens():
                for i in range(NT):
                    dve.tensor_scalar(pick[:, i, :], iota[:, :], slot_rem[:, 0, i:i + 1], None, ALU.is_equal)\
                       .then_inc(pick_half, 1)
                for i in range(NT):
                    dve.wait_ge(pick_half, pick_base + i + 1)
                    last = dve.scalar_tensor_tensor(pick[:, i, :], iota[:, :], slot_rem[:, 1, i:i + 1],
                                                    pick[:, i, :], ALU.is_equal, ALU.add)
                last.then_inc(picked, 1)
                dve.wait_ge(picked, pick_n + 1)
                dve.tensor_scalar(slot_rem, slot_rem, -float(T), None, ALU.add).then_inc(rem_ready, 1)
                dve.wait_ge(rem_ready, pick_n + 1)

            dve.wait_ge(tables_ready, 1)
            dve.wait_ge(stage_out[0], 48)
            items = dve.value_load(table[0:1, 2 * NE:2 * NE + 1], min_val=NE, max_val=MAX_ITEMS)
            pick_base, pick_n = 0, 0
            pick_tokens()
            dve.wait_ge(gathered, 1)
            pick_base, pick_n = NT, 1
            pick_tokens()
            with dve.Fori(0, items) as i:
                dve.wait_ge(sig_ready, i + 1)
                dve.tensor_tensor(hid, U, sig, ALU.mult).then_inc(hid_ready, 1)
                dve.wait_ge(gathered, i + 2)
                pick_base, pick_n = NT * i + 2 * NT, i + 2
                pick_tokens()
                dve.wait_ge(down_done, i + 1)
                for h in range(2):
                    dve.wait_ge(y_stored[h], 16 * i + 16)
                dve.tensor_copy(y_half, Y[:, :]).then_inc(y_ready, 1)

            for h in range(2):
                dve.wait_ge(y_stored[h], 16 * items + 16)
            dve.tensor_copy(small[:, 45:46], small[:, 12:13]).then_inc(all_stored, 1)
            for i in range(NT):
                for c in range(2):
                    dve.wait_ge(rows_in[2 * i + c], 16)
                    rows = (rowsA if c == 0 else rowsB)[:, i, :]
                    ins = dve.scalar_tensor_tensor(x_tok[:, i, :], rows, coef[c][:, i:i + 1], x_tok[:, i, :],
                                                   ALU.mult, ALU.add)
                    if c == 0:
                        link(ins)
                    else:
                        ins.then_inc(final_ready, 1)
            rms_scale(3 * NT, 4, small[:, 16:16 + NT], small[:, 20:20 + NT], small[:, 24:24 + NT], small[:, 28:28 + NT])
            for i in range(NT):
                dve.scalar_tensor_tensor(n_tok[:, i, :], x_tok[:, i, :], small[:, 28 + i:29 + i], gf,
                                         ALU.mult, ALU.mult).then_inc(normed, 1)

        @block.tensor
        def _(pe):
            def start_aux(a):
                if a >= 4:
                    wait_aux_read(pe, a - 4)
                return bank[4 + a % 4]

            def end_aux(ins):
                ins.then_inc(aux_done, 1)

            pe.wait_ge(consts, 6)
            pe.wait_ge(vec_in, 16 * 8)
            b = start_aux(aux("vec"))
            for m in range(KB):
                last = pe.transpose(b[:, m * NV:(m + 1) * NV], stage[0:NV, 0, m * P:(m + 1) * P], ident[0:NV, 0:NV])
            end_aux(last)
            for k in range(KB):
                b = start_aux(aux("xT", k))
                for i in range(NT):
                    pe.wait_ge(normed, i + 1)
                    last = pe.transpose(b[:, i * P:(i + 1) * P], n_tok[:, i, k * P:(k + 1) * P], ident[:, :])
                end_aux(last)
            def cached_rows():
                pe.wait_ge(cache_in, 32)
                b = start_aux(aux("ca"))
                n = NS * HA
                for m in range(KB):
                    last = pe.transpose(b[:, m * n:(m + 1) * n], stage[0:n, 1, m * P:(m + 1) * P], ident[0:n, 0:n])
                end_aux(last)
                n = NS // 2 * HB
                cache_rows = cvb[:, :, :].rearrange("p k n -> p (k n)")[:, 0:2 * D].rearrange("p (t d) -> p t d", t=2)
                for j in range(4):
                    b = start_aux(aux("cb", j))
                    for m in range(4):
                        c0 = (4 * (j % 2) + m) * P
                        last = pe.transpose(b[:, m * n:(m + 1) * n], cache_rows[0:n, j // 2, c0:c0 + P], ident[0:n, 0:n])
                    end_aux(last)

            def new_rows(t, m):
                if t == 0:
                    return ua_k[:, m, PA - HA:PA]
                if t == 1:
                    return tails[:, m, 0:NS * HA]
                if t == 2:
                    return ub_k[:, m, PB - HB:PB]
                n = NS // 2 * HB
                return tails[:, m, NS * HA + (t - 3) * n:NS * HA + (t - 2) * n]

            def split_products(b, cols, w, x, k, first, last_of_group, weights_move):
                for n, (wp, xp) in enumerate(((w[0], x[0]), (w[0], x[1]), (w[1], x[0]))):
                    start, stop = first and n == 0, last_of_group and n == 2
                    if weights_move:
                        ins = pe.matmul(b, xp[:, k, cols], wp[:, k % UK, :], start=start, stop=stop)
                    else:
                        ins = pe.matmul(b, wp[:, k % UK, cols], xp[:, k, :], start=start, stop=stop)
                return ins

            for q, (s, half) in enumerate(CHUNKS):
                groups = [i for i, x in enumerate(GROUPS) if x[2] == q]
                for h in range(2):
                    u = 2 * q + h
                    pe.wait_ge(lo_ready, u + 1)
                    ready = {"Wa": (in_lo_ready, UK * (h + 1)), "Wb": (in_lo_ready, KB + UK * (h + 1)),
                             "Wo": (merged_lo_ready, UK * (h + 1))}.get(s)
                    if ready:
                        pe.wait_ge(*ready)
                    x = {"Wa": (in_hi, cva_lo), "Wb": (in_hi, cvb_lo), "Wo": (x_hi, merged_lo)}.get(s, (x_hi, x_lo))
                    for j, g in enumerate(groups):
                        if h == 0 and g >= NBANK:
                            wait_group_read(pe, g - NBANK)
                        b = bank[g % NBANK]
                        for kk in range(UK):
                            k = h * UK + kk
                            if u == 0 and j == 0:
                                wait_aux_read(pe, aux("xT", k))
                            if u == 1 and j == 0:
                                wait_aux_read(pe, aux("xT", k))
                            last = split_products(b[:, :] if s == "Wo" else b[:, 0:N], slice(j * P, (j + 1) * P),
                                                  (w_hi[u % NW], w_lo[u % NW]), x, k, k == 0, k == KB - 1, s == "Wo")
                        if h == 1:
                            last.then_inc(grp_done, 1)
                    if h == 0:
                        last.then_inc(half_done, 1)
                if q == 1:
                    cached_rows()
                if q == NEW_AT:
                    pe.wait_ge(tails_ready, 2 * KB)
                    for a in range(aux("new", 0), aux("mean")):
                        t, h = AUX[a][1] // 2, AUX[a][1] % 2
                        b = start_aux(a)
                        for m4 in range(4):
                            last = pe.transpose(b[0:OUT_ROWS[t], m4 * P:(m4 + 1) * P], new_rows(t, 4 * h + m4),
                                                ident[:, :])
                        end_aux(last)
                if q == MEAN_AT:
                    pe.wait_ge(conv_b_ops, CONV_B_OPS)
                    b = start_aux(aux("mean"))
                    for k in range(KB):
                        last = pe.matmul(b[:, 0:N], ones[:, :], cvb[:, k, :], start=(k == 0), stop=(k == KB - 1))
                    end_aux(last)
                if q == VAR_AT:
                    pe.wait_ge(squared, KB)
                    b = start_aux(aux("var"))
                    for k in range(KB):
                        last = pe.matmul(b[:, 0:N], ones[:, :], sq[:, k, :], start=(k == 0), stop=(k == KB - 1))
                    end_aux(last)

            for k in range(KB):
                b = start_aux(aux("x2T", k))
                for i in range(NT):
                    pe.wait_ge(normed, NT + i + 1)
                    last = pe.transpose(b[:, i * P:(i + 1) * P], n_tok[:, i, k * P:(k + 1) * P], ident[:, :])
                end_aux(last)
            for a in (aux("x2T", KB - 1), aux("x2T", KB - 2)):
                wait_aux_read(pe, a)
            pe.wait_ge(rw_in, 64)
            b = start_aux(aux("logit"))
            for i in range(NT):
                for k in range(KB):
                    last = pe.matmul(b[:, i * R:(i + 1) * R], x2T[:, k, i * P:(i + 1) * P], rw[:, k, :],
                                     start=(k == 0), stop=(k == KB - 1))
            end_aux(last)
            pe.wait_ge(masks_ready, 1)
            b = start_aux(aux("pos"))
            for i in range(NT):
                for j in range(i + 1):
                    pe.matmul(b[:, i * NE:(i + 1) * NE], before[:, :] if j == i else ones[:, :], both_hot[:, j, :],
                              start=(j == 0), stop=(j == i))
            for j in range(NT):
                last = pe.matmul(b[0:NE, NT * NE:NT * NE + 1], both_hot[:, j, :], ones[:, 0:1],
                                 start=(j == 0), stop=(j == NT - 1))
            end_aux(last)
            pe.wait_ge(counts_ready, 1)
            b = start_aux(aux("table"))
            pe.matmul(b[0:1, 0:NE], ntile, ident[0:NE, 0:NE], start=True, stop=True)
            pe.matmul(b[0:1, NE:2 * NE], ntile, before[0:NE, 0:NE], start=True, stop=True)
            pe.matmul(b[0:1, 2 * NE:2 * NE + 1], ntile, ones[0:NE, 0:1], start=True, stop=True)
            end_aux(pe.matmul(b[:, 2 * NE + 1:3 * NE + 1], ntile_b, before[0:NE, 0:NE], start=True, stop=True))

            def gather(blocks):
                for k in blocks:
                    for c in range(3):
                        for i in range(NT):
                            last = pe.matmul(XE[:, k * T:(k + 1) * T], parts[c][:, i, k * P:(k + 1) * P],
                                             pick[:, i, :], start=(c == 0 and i == 0), stop=(c == 2 and i == NT - 1))
                if KB - 1 in blocks:
                    last.then_inc(gathered, 1)

            pe.wait_ge(picked, 1)
            for part in part_ready:
                pe.wait_ge(part, NT)
            wait_group_read(pe, len(GROUPS) - 1)
            gather(range(KB))

            def item(i, slots, filled):
                pe.wait_ge(xe_ready, i + 1)
                pe.wait_ge(weights_in[slots[0]], filled[0])
                pe.wait_ge(weights_in[slots[1]], filled[1])
                for k in range(KB):
                    for dst, slot in ((G, slots[0]), (U, slots[1])):
                        last = pe.matmul(dst, xe[:, k, :], wide(slot)[:, k, :], start=(k == 0), stop=(k == KB - 1))
                last.then_inc(gate_up_done, 1)
                pe.wait_ge(picked, i + 2)
                gather(range(KB // 2 - 1))
                pe.wait_ge(hid_ready, i + 1)
                gather([KB // 2 - 1])
                for k in range(HK):
                    last = pe.transpose(HT[:, k * T:(k + 1) * T], hid[:, k * P:(k + 1) * P], ident[0:T, 0:T])
                last.then_inc(hid_turned, 1)
                gather(range(KB // 2, KB))
                pe.wait_ge(hidT_ready, i + 1)
                pe.wait_ge(weights_in[slots[2]], filled[2])
                for k in range(HK):
                    for h in range(2):
                        last = pe.matmul(Y[h * T:(h + 1) * T, :], hidT[:, k, :],
                                         deep(slots[2])[:, k, h * HALF:(h + 1) * HALF],
                                         start=(k == 0), stop=(k == HK - 1))
                last.then_inc(down_done, 1)

            pe.wait_ge(tables_ready, 1)
            with pe.Fori(0, NE // 2) as pair:
                for par in range(2):
                    e = pair * 2 + par
                    n = pe.value_load(table[0:1, bass.ds(e, 1)], min_val=1, max_val=N // T)
                    first = pe.value_load(table[0:1, bass.ds(e + NE, 1)], min_val=0, max_val=MAX_ITEMS - 1)
                    slots = [3 * par + c for c in range(3)]
                    filled = [pair * 16 + 16] * 3
                    with pe.Fori(0, n) as j:
                        item(first + j, slots, filled)


_INS = ["x_prompt", "x_sample", "cache_conv_a", "cache_conv_b", "norm1_g", "w_in", "gate_b", "conv_a_w", "w_out_a",
        "conv_b_w", "conv_b_b", "ln_b_g", "ln_b_b", "w_out_b", "b_out_b", "w_o", "norm2_g", "router_group_w",
        "router_group_b", "router_expert_w", "router_expert_b", "exp_w_gate", "exp_w_up", "exp_w_down",
        "final_norm_g"]


def kernel(**inputs):
    import numpy as np
    import concourse.bacc as bacc
    from concourse.bass_utils import run_bass_kernel_spmd

    nc = bacc.Bacc("TRN2", target_bir_lowering=False, num_devices=1)
    arrays, args = {}, []
    for name in _INS:
        a = np.ascontiguousarray(inputs[name])
        arrays[f"in_{name}"] = a
        args.append(nc.dram_tensor(f"in_{name}", a.shape, mybir.dt.from_np(a.dtype), kind="ExternalInput").ap())
    xp, xs, ca, cb = (inputs[n].shape for n in _INS[:4])
    outs = [xp, xs, (ca[0], xp[0]) + tuple(ca[2:]), ca, (cb[0], xp[0]) + tuple(cb[2:]), cb]
    for i, shape in enumerate(outs):
        args.append(nc.dram_tensor(f"out_{i}", tuple(shape), F32, kind="ExternalOutput").ap())
    trunk_program(nc, *args)
    r = run_bass_kernel_spmd(nc, [arrays], core_ids=[0])
    return tuple(r.results[0][f"out_{i}"] for i in range(len(outs)))
```

```python
from contextlib import ExitStack

import concourse.bass as bass
from concourse import mybir

F32 = mybir.dt.float32
F32R = mybir.dt.float32r
I32 = mybir.dt.int32
U32 = mybir.dt.uint32
BF16 = mybir.dt.bfloat16
ALU = mybir.AluOpType
ACT = mybir.ActivationFunctionType
AX = mybir.AxisListType

P = 128


def trunk_program(nc, x_prompt, x_sample, cache_a, cache_b, norm1_g, w_in, gate_b, conv_a_w, w_out_a, conv_b_w,
                  conv_b_b, ln_b_g, ln_b_b, w_out_b, b_out_b, w_o, norm2_g, group_w, group_b, expert_w, expert_b,
                  w_gate, w_up, w_down, final_g, y_prompt, y_sample, new_a_prompt, new_a_sample, new_b_prompt,
                  new_b_sample):
    D = x_prompt.shape[2]
    NP = x_prompt.shape[1]
    NS, TS = x_sample.shape[0], x_sample.shape[1]
    N = NP + NS * TS
    NT = N // P
    KB = D // P
    KA_TAPS, KB_TAPS = conv_a_w.shape[1], conv_b_w.shape[1]
    HA, HB = KA_TAPS - 1, KB_TAPS - 1
    NE, DE = w_gate.shape[1], w_gate.shape[3]
    NG = group_w.shape[2]
    EPG = NE // NG
    HK = DE // P
    T = 64
    TQ = T // 2
    QE = DE // 2
    HALF = 512
    RING = 6
    MAX_ITEMS = NE + 2 * N // T
    R = NG + NE
    BIG = 1.0e30

    PA = HA + NP
    SA = HA + TS
    PB, SB = HB + NP, HB + TS
    WA, WB = PA + NS * SA, PB + NS * SB

    SECTION = {"B": 0, "C": 1, "H": 2, "GA": 3, "GB": 4, "gA": 5, "gB": 6}
    CHUNKS = [("GB", 0), ("GA", 0), ("GB", 1), ("GA", 1), ("C", 0), ("H", 0), ("C", 1), ("H", 1), ("B", 0),
              ("B", 1), ("Wa", 0), ("Wa", 1), ("gA", 0), ("gA", 1), ("gB", 0), ("gB", 1), ("Wb", 0), ("Wb", 1),
              ("Wo", 0), ("Wo", 1)]
    NCH = len(CHUNKS)
    GROUPS = []
    for q, (s, half) in enumerate(CHUNKS):
        for j in range(NT if s == "Wo" else HALF // P):
            GROUPS.append((s, j if s == "Wo" else half * (HALF // P) + j, q))
    UNITS = 2 * NCH
    UK = KB // 2
    NW = 3
    BY_ACT = ("GB", "C", "Wa", "gA", "gB")
    CHUNK_END = [1 + max(i for i, x in enumerate(GROUPS) if x[2] == q) for q in range(NCH)]
    NBANK = 4

    def group(s, m):
        return [i for i, x in enumerate(GROUPS) if x[0] == s and x[1] == m][0]

    AUX = [("vec", 0, "dve")]
    AUX += [("xT", k, "dve") for k in range(KB)]
    AUX += [("ca", 0, "dve")]
    AUX += [("cb", j, "act") for j in range(4)]
    OUT_TILES = ["ap", "as", "bp", "bs0", "bs1"]
    AUX += [("new", j, "act") for j in range(2 * len(OUT_TILES))]
    AUX += [("mean", 0, "dve"), ("var", 0, "dve")]
    AUX += [("x2T", j, "act" if j % 2 else "dve") for j in range(2 * NT)]
    AUX += [("logit", i, "dve") for i in range(NT)]
    AUX += [("pos", 0, "dve"), ("table", 0, "dve"), ("quarters", 0, "dve")]
    AUX += [("spread", j, "act") for j in range(4)]

    HEAD = 6
    PRODUCTS = {q: [] for q in range(NCH)}
    head = [("b", m, tap) for tap in range(1, HEAD) for m in range(KB // 2, KB)]
    for q, n in ((4, 8), (5, 8), (7, 4)):
        PRODUCTS[q] += [head.pop(0) for _ in range(n)]
    assert not head
    PRODUCTS[6] = [("a", m, tap) for m in range(KB // 2) for tap in range(1, KA_TAPS)]
    for q in (8, 9):
        PRODUCTS[q] = [("a", m, tap) for m in range(2 * q - 12, 2 * q - 10) for tap in range(1, KA_TAPS)]
    NPS = 4
    SLICES = {2: 4, 3: 5, 4: 4, 5: 5, 6: 4, 7: 5, 8: 4, 9: 5, 10: 5, 11: 5, 12: 5, 13: 5}
    MEAN_AT, VAR_AT, NEW_AT = 13, 14, 9

    def aux(name, j=0):
        return AUX.index([a for a in AUX if a[0] == name and a[1] == j][0])

    V_N1, V_GATE, V_CA, V_CB = 0, 1, 3, 3 + KA_TAPS
    V_CBB = V_CB + KB_TAPS
    V_LNG, V_LNB, V_BO, V_N2 = V_CBB + 1, V_CBB + 2, V_CBB + 3, V_CBB + 4
    NV = V_N2 + 1

    with ExitStack() as ctx:
        def sb(name, shape, dt=F32):
            return ctx.enter_context(nc.sbuf_tensor(name, shape, dt))

        def sem(name):
            return ctx.enter_context(nc.semaphore(name))

        bank = [ctx.enter_context(nc.psum_tensor(f"bank{i}", [P, 512], F32)) for i in range(8)]
        arena_at = -(-nc.sbuf_base // 32) * 32
        arena = sb("arena", [P, RING * 4096])
        same_at = -(-nc.sbuf_base // 32) * 32
        same = sb("same", [P, 4 * KB * N])

        def at(name, shape, dt, offset):
            return nc.alloc_sbuf_tensor_at(name, shape, dt, offset=offset)

        UNIT = 4 * UK * HALF
        ACTS = 4 * KB * N
        ring = [at(f"ring{i}", [P, 4096], F32, arena_at + 2 * UNIT * i) for i in range(RING)]
        raw = [at(f"raw{i}", [P, UK, HALF], F32, arena_at + UNIT * i) for i in range(NW)]
        w_hi = [at(f"w_hi{i}", [P, UK, HALF], F32R, arena_at + UNIT * (NW + i)) for i in range(NW)]
        w_lo = [at(f"w_lo{i}", [P, UK, HALF], F32R, arena_at + UNIT * (2 * NW + i)) for i in range(NW)]
        x_lo = at("x_lo", [P, KB, N], F32R, arena_at + 3 * NW * UNIT)
        in_hi = at("in_hi", [P, KB, N], F32R, arena_at + 3 * NW * UNIT + ACTS)
        assert 3 * NW * UNIT + 2 * ACTS <= RING * 2 * UNIT
        x_hi = at("x_hi", [P, KB, N], F32R, same_at)
        x2T = at("x2T", [P, KB, N], F32, same_at)
        cva = at("cva", [P, KB, N], F32, same_at + ACTS)
        cva_lo = at("cva_lo", [P, KB, N], F32R, same_at + ACTS)
        cvb = at("cvb", [P, KB, N], F32, same_at + 2 * ACTS)
        cvb_lo = at("cvb_lo", [P, KB, N], F32R, same_at + 2 * ACTS)
        n_tok = at("n_tok", [P, NT, D], F32, same_at + 3 * ACTS)
        merged = at("merged", [P, KB, N], F32, same_at + 3 * ACTS)
        merged_lo = at("merged_lo", [P, KB, N], F32R, same_at + 3 * ACTS)
        back_to = at("back_to", [P, N], F32R, same_at + ACTS + 4 * 4 * N)
        x_tok = sb("x_tok", [P, NT, D])
        tails = n_tok[:, :, :].rearrange("p t d -> p (t d)")[:, 0:KB * NS * (HA + HB)].rearrange(
            "p (k n) -> p k n", k=KB)
        ua = sb("ua", [P, KB * WA])
        ub = sb("ub", [P, KB * WB])
        tmp = sb("tmp", [P, HALF // P, N])
        stage_at = -(-nc.sbuf_base // 32) * 32
        stage = sb("stage", [P, 2, D])
        y_hi = at("y_hi", [P, D], F32R, stage_at)
        y_lo = at("y_lo", [P, D], F32R, stage_at + 4 * D)
        product = stage[:, :, :].rearrange("p a d -> p (a d)")[:, 0:NPS * N].rearrange("p (s n) -> p s n", s=NPS)
        vec = sb("vec", [P, KB, NV])
        ident = sb("ident", [P, P])
        ones = sb("ones", [P, P])
        ones_b = sb("ones_b", [P, P], BF16)
        before_b = sb("before_b", [P, P], BF16)
        table_sums = sb("table_sums", [NE, 2 * NE + 1], BF16)
        steps = sb("steps", [NE, N // TQ - 1])
        iota = sb("iota", [P, T])
        small = sb("small", [P, 48])
        mark = small[:, 36:36 + 6]
        zero = sb("zero", [1, 4])
        own_slot = sb("own_slot", [P, 3])
        coef_part = sb("coef_part", [P, 2])
        slot_coef = sb("slot_coef", [P, 2])
        rbias = sb("rbias", [P, R])[:, :]
        down_rank = sb("down_rank", [P, NE])[:, :]
        table = sb("table", [1, 4 * NE + 2], I32)
        pairs_before = sb("pairs_before", [1, NE + 2])[:, :]

        ua_k = ua[:, :].rearrange("p (k n) -> p k n", k=KB)
        ub_k = ub[:, :].rearrange("p (k n) -> p k n", k=KB)

        def ua_new(m, tap):
            s = ua_k[:, m, PA:WA].rearrange("p (s n) -> p s n", s=NS)
            return ua_k[:, m, tap:tap + NP], s[:, :, tap:tap + TS]

        def ub_new(m, tap):
            s = ub_k[:, m, PB:WB].rearrange("p (s n) -> p s n", s=NS)
            return ub_k[:, m, tap:tap + NP], s[:, :, tap:tap + TS]

        def both(t):
            return t[:, 0:NP], t[:, NP:N].rearrange("p (s n) -> p s n", s=NS)

        sq = ua[:, 0:KB * N].rearrange("p (k n) -> p k n", k=KB)
        gf = ub[:, D:2 * D]
        junk = ub[:, 2 * D:3 * D]
        rw = ub[:, 3 * D:3 * D + KB * R].rearrange("p (k r) -> p k r", k=KB)
        ua_b, cva_b = ua[:, :].bitcast(BF16), cva[:, :, :].rearrange("p k n -> p (k n)").bitcast(BF16)
        parts = [x.rearrange("p (i d) -> p i d", d=D) for x in
                 (ua_b[:, 0:NT * D], ua_b[:, NT * D:2 * NT * D], cva_b[:, 0:NT * D])]
        pick = cvb[:, 0, 0:NT * T // 2].bitcast(BF16).rearrange("p (i t) -> p i t", i=NT)
        xe = cvb[:, 1:3, :].rearrange("p k n -> p (k n)")[:, 0:KB * T].rearrange("p (k t) -> p k t", k=KB)
        sig = cvb[:, 3:5, :].rearrange("p k n -> p (k n)")[T:2 * T, 0:DE]
        hid = cvb[:, 5:7, :].rearrange("p k n -> p (k n)")[0:T, 0:DE]
        hidT = cvb[:, 7, 0:HK * T].rearrange("p (k t) -> p k t", k=HK)
        diagonal = x2T[:, 0:4, :]
        spread_rows = x2T[:, 4:8, :]
        at_slot = cva[:, 5:7, :]
        rt = tmp[:, :, :].rearrange("p k n -> p (k n)")
        cols = [0]

        def scratch(n, rows=P):
            a = rt[0:rows, cols[0]:cols[0] + n]
            cols[0] += n
            return a

        x_in = sem("x_in")
        vec_in = sem("vec_in")
        cache_in = sem("cache_in")
        rw_in = sem("rw_in")
        rw_scaled = sem("rw_scaled")
        rstd_ready = sem("rstd_ready")
        g_in = sem("g_in")
        unit_in = [sem(f"unit_in{i}") for i in range(NW)]
        hi_ready = sem("hi_ready")
        lo_ready = sem("lo_ready")
        half_done = sem("half_done")
        x_hi_ready = sem("x_hi_ready")
        conv_first = sem("conv_first")
        product_ready = sem("product_ready")
        product_added = sem("product_added")
        in_hi_ready = sem("in_hi_ready")
        in_lo_ready = sem("in_lo_ready")
        v_done = sem("v_done")
        added = sem("added")
        merged_hi_ready = sem("merged_hi_ready")
        merged_lo_ready = sem("merged_lo_ready")
        weights_in = [[sem(f"weights_in{i}_{h}") for h in range(2)] for i in range(RING)]
        consts = sem("consts")
        zero_ready = sem("zero_ready")
        hist_zero = sem("hist_zero")
        ssq_ready = sem("ssq_ready")
        root_in = sem("root_in")
        root_out = sem("root_out")
        normed = sem("normed")
        grp_done = sem("grp_done")
        act_grp = sem("act_grp")
        dve_grp = sem("dve_grp")
        aux_done = sem("aux_done")
        act_aux = sem("act_aux")
        dve_aux = sem("dve_aux")
        conv_b_ops = sem("conv_b_ops")
        dve_chain = sem("dve_chain")
        centred = sem("centred")
        squared = sem("squared")
        blocks_summed = sem("blocks_summed")
        scaled = sem("scaled")
        gate_a_merged = sem("gate_a_merged")
        stage_out = [sem(f"stage_out{i}") for i in range(2)]
        tails_ready = sem("tails_ready")
        masks_ready = sem("masks_ready")
        exp_in = sem("exp_in")
        exp_out = sem("exp_out")
        counts_ready = sem("counts_ready")
        tables_ready = sem("tables_ready")
        picked = sem("picked")
        pick_half = sem("pick_half")
        rem_ready = sem("rem_ready")
        gathered = sem("gathered")
        xe_ready = sem("xe_ready")
        gate_up_clear = sem("gate_up_clear")
        gate_up_half = sem("gate_up_half")
        gate_up_done = sem("gate_up_done")
        hid_turned = sem("hid_turned")
        hidT_ready = sem("hidT_ready")
        part_ready = [sem(f"part{i}_ready") for i in range(3)]
        rest_ready = sem("rest_ready")
        sig_ready = sem("sig_ready")
        hid_ready = sem("hid_ready")
        down_half = sem("down_half")
        down_done = sem("down_done")
        y_ready = sem("y_ready")
        slots_ready = sem("slots_ready")
        coefs_ready = sem("coefs_ready")
        diagonal_ready = sem("diagonal_ready")
        own_slot_ready = sem("own_slot_ready")
        back_part = sem("back_part")
        coef_half = sem("coef_half")
        slot_coef_ready = sem("slot_coef_ready")
        y_hi_ready = sem("y_hi_ready")
        back_ready = sem("back_ready")
        combined = sem("combined")
        tile_added = sem("tile_added")
        y_out = sem("y_out")

        def wait_group_read(eng, g):
            by_act = GROUPS[g][0] in BY_ACT
            n = sum((x[0] in BY_ACT) == by_act for x in GROUPS[:g + 1])
            eng.wait_ge(act_grp if by_act else dve_grp, n)

        def wait_aux_read(eng, a):
            n = sum(x[2] == AUX[a][2] for x in AUX[:a + 1])
            eng.wait_ge(act_aux if AUX[a][2] == "act" else dve_aux, n)

        def wait_unit_used(eng, u):
            if u % 2:
                eng.wait_ge(grp_done, CHUNK_END[u // 2])
            else:
                eng.wait_ge(half_done, u // 2 + 1)

        def product_number(kind, m, tap):
            order = [x for q in range(NCH) for x in PRODUCTS[q]]
            return order.index((kind, m, tap)) + 1

        w_in_k = w_in.rearrange("l (k p) c -> p (l k) c", p=P)
        w_sq = {"Wa": w_out_a.rearrange("l (k p) c -> p (l k) c", p=P),
                "Wb": w_out_b.rearrange("l (k p) c -> p (l k) c", p=P),
                "Wo": w_o.rearrange("l (k p) c -> p (l k) c", p=P)}
        w_gu = {0: w_gate.rearrange("l e (k p) c -> (l e) p k c", p=P), 1: w_up.rearrange("l e (k p) c -> (l e) p k c", p=P)}
        w_dn = w_down.rearrange("l e (k p) c -> (l e) p k c", p=P)

        def wide(slot):
            return ring[slot][:, :].rearrange("p (k c) -> p k c", k=KB)

        def deep(slot):
            return ring[slot][:, :].rearrange("p (k c) -> p k c", k=HK)

        lg = scratch(NT * R).rearrange("p (i r) -> p i r", i=NT)
        gmax = scratch(NT)
        ghot = scratch(NT * NG).rearrange("p (i g) -> p i g", i=NT)
        gexp = scratch(NT * NG).rearrange("p (i g) -> p i g", i=NT)
        le = scratch(NT * NE).rearrange("p (i e) -> p i e", i=NT)
        hots = scratch(2 * NT * NE).rearrange("p (c i e) -> p c i e", c=2, i=NT)
        hot = [hots[:, c] for c in range(2)]
        hot_slots = scratch(2 * NT * NE).rearrange("p (c i e) -> p c i e", c=2, i=NT)
        both_b = scratch(NT * NE // 2).bitcast(BF16).rearrange("p (i e) -> p i e", i=NT)
        ntile_b = scratch(P // 2, NE).bitcast(BF16)
        t0 = scratch(NT * NE).rearrange("p (i e) -> p i e", i=NT)
        t1 = scratch(NT * NE).rearrange("p (i e) -> p i e", i=NT)
        top = [scratch(NT) for _ in range(2)]
        dexp = scratch(NT)
        coef = [scratch(NT) for _ in range(2)]
        psum_g = scratch(NT)
        slot_f = scratch(2 * NT).rearrange("p (c i) -> p c i", c=2)
        slot_rem = scratch(2 * NT).rearrange("p (c i) -> p c i", c=2)
        cnt = scratch(1, NE)
        more = scratch(1, NE)
        more_each = scratch(N // TQ - 1, NE)
        quarters_b = scratch(P // 2, NE).bitcast(BF16)
        assert cols[0] <= 4 * N

        OUT_ROWS = [HA, NS * HA, HB, NS // 2 * HB, NS // 2 * HB]
        nbs = new_b_sample.rearrange("l s h d -> (l s h) d")
        OUT_DST = [new_a_prompt.rearrange("l b h d -> (l b h) d"), new_a_sample.rearrange("l s h d -> (l s h) d"),
                   new_b_prompt.rearrange("l b h d -> (l b h) d"), nbs[0:NS // 2 * HB, :], nbs[NS // 2 * HB:, :]]
        OWN_FIRST = 3 + P // TQ
        PRODUCT_COUNT = sum(len(x) for x in PRODUCTS.values())
        CONV_B_OPS = KB * (2 * KB_TAPS - HEAD)
        ACT_AUX_NEW = sum(x[2] == "act" for x in AUX[:aux("mean")])
        WO_LAST = [[i for i, x in enumerate(GROUPS) if x == ("Wo", t, NCH - 1)][0] for t in range(NT)]
        XE = bank[0][:, 0:KB * T]
        HT = bank[2][:, 0:HK * T]
        Y = bank[3]

        def gate_and_up(second):
            return bank[1 + second][:, second * QE:(second + 1) * QE]

        def back(t):
            return bank[4 + 2 * (t % 2)], bank[5 + 2 * (t % 2)]

        block = ctx.enter_context(nc.Block())

        @block.sync
        def _(sp):
            sp.dma_start(x_tok[:, 0:NP // P, :], x_prompt[0].rearrange("(i p) d -> p i d", p=P)).then_inc(x_in, 16)
            sp.dma_start(x_tok[:, NP // P, :], x_sample.rearrange("s t d -> (s t) d")).then_inc(x_in, 16)
            for u in range(UNITS):
                if u == 1:
                    sp.wait_ge(vec_in, 16 * 9)
                (s, half), k0 = CHUNKS[u // 2], u % 2 * UK
                if u >= NW:
                    sp.wait_ge(lo_ready, u - NW + 1)
                w, c0 = (w_sq[s], half * HALF) if s in w_sq else (w_in_k, SECTION[s] * D + half * HALF)
                sp.dma_start(raw[u % NW][:, :, :], w[:, k0:k0 + UK, c0:c0 + HALF]).then_inc(unit_in[u % NW], 16)

            def expert_weights(e, par, first):
                for c, h in ((0, 0), (1, 0), (0, 1), (1, 1), (2, 0), (2, 1)):
                    slot = 3 * par + c
                    if first:
                        sp.wait_ge(lo_ready, UNITS)
                        if slot:
                            sp.wait_ge(grp_done, len(GROUPS))
                    else:
                        used = (down_half, down_done) if c == 2 else (gate_up_half, gate_up_done)
                        sp.wait_ge(used[h], last_item)
                    dst, src = (deep(slot), w_dn) if c == 2 else (wide(slot), w_gu[c])
                    n = (HK if c == 2 else KB) // 2
                    blocks = slice(h * n, (h + 1) * n)
                    sp.dma_start(dst[:, blocks, :], src[e, :, blocks, :] if first else
                                 src[bass.ds(e, 1), :, blocks, :].rearrange("e p k c -> p (e k) c"))\
                      .then_inc(weights_in[slot][h], 16)

            expert_weights(0, 0, True)
            expert_weights(1, 1, True)
            sp.wait_ge(tables_ready, 3)
            with sp.Fori(1, NE // 2) as pair:
                for par in range(2):
                    last_item = sp.value_load(table[0:1, bass.ds(pair * 2 + (NE + par - 1), 1)], min_val=1, max_val=MAX_ITEMS)
                    expert_weights(pair * 2 + par, par, False)

        @block.gpsimd
        def _(pool):
            pool.memset(zero[:], 0.0).then_inc(zero_ready, 1)
            pool.memset(ident[:], 0.0).then_inc(consts, 1)
            pool.memset(ones[:], 1.0).then_inc(consts, 1)
            pool.memset(ones_b[:], 1.0).then_inc(consts, 1)
            pool.wait_ge(consts, 3)
            pool.iota(own_slot[:], pattern=[[0, 3]], base=0, channel_multiplier=1,
                      allow_small_or_imprecise_dtypes=True).then_inc(consts, 1)
            pool.affine_select(out=ident[:], in_=ident[:], pattern=[[1, P]], compare_op=ALU.not_equal, fill=1.0,
                               base=0, channel_multiplier=-1).then_inc(consts, 1)
            pool.affine_select(out=before_b[:], in_=ones_b[:], pattern=[[1, P]], compare_op=ALU.is_gt, fill=0.0,
                               base=0, channel_multiplier=-1).then_inc(consts, 1)
            pool.iota(iota[:], pattern=[[1, T]], base=0, channel_multiplier=0,
                      allow_small_or_imprecise_dtypes=True).then_inc(consts, 1)
            pool.iota(down_rank, pattern=[[-1, NE]], base=NE, channel_multiplier=0,
                      allow_small_or_imprecise_dtypes=True).then_inc(consts, 1)
            pool.iota(pairs_before.rearrange("a (p s) -> a p s", s=2), pattern=[[1, NE // 2 + 1], [1, 2]], base=0,
                      channel_multiplier=0, allow_small_or_imprecise_dtypes=True).then_inc(consts, 1)
            pool.iota(steps[:], pattern=[[TQ, N // TQ - 1]], base=TQ, channel_multiplier=0,
                      allow_small_or_imprecise_dtypes=True).then_inc(consts, 1)
            pool.wait_ge(consts, 10)
            for dst, src in ((table_sums[:, 0:NE], ident[0:NE, 0:NE]),
                             (table_sums[:, NE:2 * NE], before_b[0:NE, 0:NE]),
                             (table_sums[:, 2 * NE:], ones[0:NE, 0:1])):
                pool.tensor_copy(dst, src).then_inc(consts, 1)
            pool.memset(ua_k[:, :, 0:HA], 0.0).then_inc(hist_zero, 1)
            pool.memset(ub_k[:, :, 0:HB], 0.0).then_inc(hist_zero, 1)
            def low_part(u):
                pool.wait_ge(hi_ready, u + 1)
                if u >= NW:
                    wait_unit_used(pool, u - NW)
                pool.tensor_tensor(w_lo[u % NW][:, :, :], raw[u % NW][:, :, :], w_hi[u % NW][:, :, :].bitcast(F32),
                                   ALU.subtract).then_inc(lo_ready, 1)

            low_part(0)
            low_part(1)
            for q, (s, half) in enumerate(CHUNKS):
                if 2 * q + 2 < UNITS:
                    low_part(2 * q + 2)
                todo = PRODUCTS[q]
                for n, (kind, m, tap) in enumerate(todo):
                    if n == len(todo) // 2:
                        low_part(2 * q + 3)
                    at_n = product_number(kind, m, tap)
                    pool.wait_ge(product_ready, at_n)
                    if tap > 1:
                        pool.wait_ge(product_added, product_number(kind, m, tap - 1))
                    cv = (cva if kind == "a" else cvb)[:, m, :]
                    pool.tensor_tensor(cv, cv, product[:, (at_n - 1) % NPS, :], ALU.add).then_inc(product_added, 1)
                if q == VAR_AT + 1:
                    for m in range(KB):
                        pool.wait_ge(in_hi_ready, KB + m + 1)
                        pool.tensor_tensor(cvb_lo[:, m, :], cvb[:, m, :], in_hi[:, m, :].bitcast(F32), ALU.subtract)\
                            .then_inc(in_lo_ready, 1)
                if 2 * q + 3 < UNITS and not todo:
                    low_part(2 * q + 3)
                for m in range(4 * half, 4 * half + 4):
                    if s == "B":
                        pool.wait_ge(in_hi_ready, m + 1)
                        pool.tensor_tensor(cva_lo[:, m, :], cva[:, m, :], in_hi[:, m, :].bitcast(F32), ALU.subtract)\
                            .then_inc(in_lo_ready, 1)
                    elif s == "gA":
                        wait_group_read(pool, group("gA", m))
                        pool.tensor_tensor(merged[:, m, :], merged[:, m, :], tmp[:, m % 4, :], ALU.mult)\
                            .then_inc(gate_a_merged, 1)
                    elif s == "Wb":
                        pool.wait_ge(merged_hi_ready, m + 1)
                        pool.tensor_tensor(merged_lo[:, m, :], merged[:, m, :], x_hi[:, m, :].bitcast(F32),
                                           ALU.subtract).then_inc(merged_lo_ready, 1)
            pool.wait_ge(stage_out[0], 48)
            pool.wait_ge(stage_out[1], 32)
            pool.memset(y_hi[:].bitcast(F32), 0.0).then_inc(y_ready, 1)
            pool.memset(y_lo[:].bitcast(F32), 0.0).then_inc(y_ready, 1)
            pool.memset(back_to[:].bitcast(F32), 0.0).then_inc(back_ready, 1)
            for i in range(NT):
                pool.wait_ge(part_ready[0], i + 1)
                pool.wait_ge(normed, NT + i + 1)
                pool.tensor_tensor(n_tok[:, i, :], n_tok[:, i, :], parts[0][:, i, :], ALU.subtract)\
                    .then_inc(rest_ready, 1)
            for i in range(NT - 1):
                pool.wait_ge(part_ready[1], i + 1)
                pool.tensor_tensor(parts[2][:, i, :], n_tok[:, i, :], parts[1][:, i, :], ALU.subtract)\
                    .then_inc(part_ready[2], 1)

        @block.scalar
        def _(act):
            def load_root_table(n):
                act.activation(zero[:, n:n + 1], zero[:, 0:1], ACT.Sqrt)

            act.wait_ge(zero_ready, 1)
            load_root_table(1)
            rows = [(V_N1, norm1_g), (V_GATE, gate_b.rearrange("l (a d) -> (l a) d", d=D)),
                    (V_CA, conv_a_w.rearrange("l k d -> (l k) d")), (V_CB, conv_b_w.rearrange("l k d -> (l k) d")),
                    (V_CBB, conv_b_b), (V_LNG, ln_b_g), (V_LNB, ln_b_b), (V_BO, b_out_b), (V_N2, norm2_g)]
            for r, src in rows:
                act.dma_start(stage[r:r + src.shape[0], 0, :], src).then_inc(vec_in, 16)
            act.wait_ge(x_in, 32)
            for i in range(NT - 1):
                act.activation(cva[:, :, :].rearrange("p k n -> p (k n)")[:, i * D:(i + 1) * D], x_tok[:, i, :],
                               ACT.Square, accum_out=small[:, i:i + 1]).then_inc(ssq_ready, 1)
            act.wait_ge(root_in, 1)
            act.activation(small[:, 8:8 + NT], small[:, 4:4 + NT], ACT.Sqrt).then_inc(root_out, 1)

            def read_aux(a):
                name, j, eng = AUX[a]
                if eng != "act":
                    return
                b = bank[4 + a % 4]
                act.wait_ge(aux_done, a + 1)
                if name == "cb":
                    t, mh = j // 2, j % 2
                    for m in range(4):
                        dst = ub_k[:, 4 * mh + m, PB:WB].rearrange("p (s n) -> p s n", s=NS)[
                            :, 4 * t:4 * t + 4, 0:HB]
                        src = b[:, m * 4 * HB:(m + 1) * 4 * HB].rearrange("p (s n) -> p s n", s=4)
                        last = act.activation(dst, src, ACT.Copy)
                    last.then_inc(act_aux, 1)
                elif name == "new":
                    t, half = j // 2, j % 2
                    n = OUT_ROWS[t]
                    if t < 2 and half == 0:
                        wait_aux_read(act, aux("ca"))
                    if t >= 2 and half == 0:
                        act.wait_ge(stage_out[t % 2], 16 * (t // 2))
                    act.activation(stage[0:n, t % 2, half * 512:(half + 1) * 512], b[0:n, :], ACT.Copy)\
                       .then_inc(act_aux, 1)
                    if half == 1:
                        wait_aux_read(act, a)
                        act.dma_start(OUT_DST[t], stage[0:n, t % 2, :]).then_inc(stage_out[t % 2], 16)
                elif name == "x2T":
                    t, h = j // 2, j % 2
                    act.activation(x2T[:, 4 * h:4 * h + 4, t * P:(t + 1) * P],
                                   b[:, :].rearrange("p (k n) -> p k n", k=4), ACT.Copy).then_inc(act_aux, 1)
                elif name == "spread":
                    act.activation(spread_rows[:, j, :], b[:, 0:N], ACT.Copy).then_inc(act_aux, 1)

            def high_part(u):
                act.wait_ge(unit_in[u % NW], 16 * (u // NW + 1))
                if u >= NW:
                    wait_unit_used(act, u - NW)
                act.activation(w_hi[u % NW][:, :, :], raw[u % NW][:, :, :], ACT.Copy).then_inc(hi_ready, 1)

            high_part(0)
            act.wait_ge(dve_aux, 1)
            for k in range(KB):
                a = aux("xT", k)
                act.wait_ge(aux_done, a + 1)
                act.activation(x_hi[:, k, :], bank[4 + a % 4][:, 0:N], ACT.Copy, scale=vec[:, k, V_N1:V_N1 + 1])\
                   .then_inc(x_hi_ready, 1)
            high_part(1)
            act.wait_ge(unit_in[1], 16)
            act.dma_start(stage[0:NS * HA, 1, :], cache_a.rearrange("l s h d -> (l s h) d")).then_inc(cache_in, 16)
            act.dma_start(cvb[0:NS // 2 * HB, :, :].rearrange("p k n -> p (k n)")[:, 0:2 * D].rearrange(
                "p (t d) -> p t d", t=2), cache_b.rearrange("l (t s) h d -> (l s h) t d", t=2))\
                .then_inc(cache_in, 16)

            def form_product(kind, m, tap):
                n = product_number(kind, m, tap)
                if n > NPS:
                    act.wait_ge(product_added, n - NPS)
                src, v = (ua_new, V_CA) if kind == "a" else (ub_new, V_CB)
                for x, y in zip(src(m, tap), both(product[:, (n - 1) % NPS, :])):
                    last = act.activation(y, x, ACT.Copy, scale=vec[:, m, v + tap:v + tap + 1])
                last.then_inc(product_ready, 1)

            def high_in(m, src):
                act.activation(in_hi[:, m, :], src, ACT.Copy).then_inc(in_hi_ready, 1)

            for q, (s, half) in enumerate(CHUNKS):
                if 2 * q + 2 < UNITS:
                    high_part(2 * q + 2)
                if q == 4:
                    wait_group_read(act, group("GA", KB - 1))
                    for m in range(KB // 2, KB):
                        for x, y in zip(ub_new(m, 0), both(cvb[:, m, :])):
                            last = act.activation(y, x, ACT.Identity, scale=vec[:, m, V_CB:V_CB + 1],
                                                  bias=vec[:, m, V_CBB:V_CBB + 1])
                        last.then_inc(conv_first, 1)
                if q in (6, 8):
                    for m in range(2 * q - 12, 2 * q - 8):
                        wait_group_read(act, group("H", m))
                        for x, y in zip(ua_new(m, 0), both(cva[:, m, :])):
                            last = act.activation(y, x, ACT.Copy, scale=vec[:, m, V_CA:V_CA + 1])
                        last.then_inc(conv_first, 1)
                todo = PRODUCTS[q]
                for n, x in enumerate(todo):
                    if n == len(todo) // 2:
                        high_part(2 * q + 3)
                    form_product(*x)
                if not todo and 2 * q + 3 < UNITS and q != VAR_AT + 1:
                    high_part(2 * q + 3)
                if q == NEW_AT:
                    wait_group_read(act, group("H", KB - 1))
                    for m in range(KB):
                        for src, first, last_col, h in ((ua_k[:, m, PA:WA], 0, SA, HA),
                                                        (ub_k[:, m, PB:WB], NS * HA, SB, HB)):
                            act.activation(
                                tails[:, m, first:first + NS * h].rearrange("p (s n) -> p s n", s=NS),
                                src.rearrange("p (s n) -> p s n", s=NS)[:, :, last_col - h:last_col],
                                ACT.Copy).then_inc(tails_ready, 1)
                if q == VAR_AT:
                    act.wait_ge(root_in, 2)
                    act.activation(sq[:, 0, :], sq[:, 1, :], ACT.Sqrt).then_inc(root_out, 1)
                if q == VAR_AT + 1:
                    for k in range(KB):
                        act.wait_ge(scaled, k + 1)
                        act.activation(cvb[:, k, :], cvb[:, k, :], ACT.Silu, scale=vec[:, k, V_LNG:V_LNG + 1],
                                       bias=vec[:, k, V_LNB:V_LNB + 1]).then_inc(v_done, 1)
                        act.wait_ge(v_done, k + 1)
                        high_in(k, cvb[:, k, :])
                    high_part(2 * q + 3)
                for g in [i for i, x in enumerate(GROUPS) if x[2] == q]:
                    m = GROUPS[g][1]
                    if q == NEW_AT and m == KB - 1:
                        act.wait_ge(product_added, PRODUCT_COUNT)
                        for a in range(aux("new", 0), aux("mean")):
                            read_aux(a)
                    b = bank[g % NBANK][:, 0:N]
                    if s in BY_ACT:
                        act.wait_ge(grp_done, g + 1)
                    if s == "GB":
                        if m >= 4:
                            wait_group_read(act, group("GA", m - 4))
                        act.activation(tmp[:, m % 4, :], b, ACT.Sigmoid).then_inc(act_grp, 1)
                    elif s == "C":
                        wait_group_read(act, group("GA", m + 4) if m < 4 else group("H", m - 4))
                        act.activation(tmp[:, m % 4, :], b, ACT.Copy).then_inc(act_grp, 1)
                    elif s == "Wa":
                        if m == 0:
                            act.wait_ge(aux_done, aux("mean"))
                        act.activation(merged[:, m, :], b, ACT.Copy).then_inc(act_grp, 1)
                    elif s == "gA":
                        if m < 4:
                            wait_group_read(act, group("H", m + 4))
                        else:
                            act.wait_ge(gate_a_merged, m - 3)
                        act.activation(tmp[:, m % 4, :], b, ACT.Sigmoid, bias=vec[:, m, V_GATE:V_GATE + 1])\
                           .then_inc(act_grp, 1)
                    elif s == "gB":
                        act.activation(cva[:, m, :], b, ACT.Sigmoid, bias=vec[:, m, V_GATE + 1:V_GATE + 2])\
                           .then_inc(act_grp, 1)
                    elif s == "B":
                        wait_group_read(act, g)
                        high_in(m, cva[:, m, :])
                    elif s == "Wb":
                        act.wait_ge(added, m + 1)
                        act.activation(x_hi[:, m, :], merged[:, m, :], ACT.Copy).then_inc(merged_hi_ready, 1)
                if q == MEAN_AT:
                    for k in range(KB):
                        act.wait_ge(centred, k + 1)
                        act.activation(sq[:, k, :], cvb[:, k, :], ACT.Square).then_inc(squared, 1)
                if q == 1:
                    for a in range(aux("ca"), aux("new", 0)):
                        read_aux(a)
            act.wait_ge(conv_b_ops, CONV_B_OPS)
            act.wait_ge(act_aux, ACT_AUX_NEW)
            act.dma_start(gf, final_g.rearrange("(a d) -> a d", a=1).to_broadcast([P, D])).then_inc(g_in, 16)
            act.dma_start(rw[:, :, 0:NG], group_w.rearrange("l (k p) g -> p (l k) g", p=P)).then_inc(rw_in, 16)
            act.dma_start(rw[:, :, NG:R], expert_w.rearrange("l (k p) g -> p (l k) g", p=P)).then_inc(rw_in, 16)
            act.dma_start(rbias[:, 0:NG], group_b.to_broadcast([P, NG])).then_inc(rw_in, 16)
            act.dma_start(rbias[:, NG:R], expert_b.to_broadcast([P, NE])).then_inc(rw_in, 16)
            load_root_table(2)
            for i in range(NT):
                read_aux(aux("x2T", 2 * i + 1))
                wait_group_read(act, WO_LAST[i])
                if i:
                    act.wait_ge(ssq_ready, NT + i)
                act.activation(junk, x_tok[:, i, :], ACT.Square, accum_out=small[:, i:i + 1]).then_inc(ssq_ready, 1)
            act.wait_ge(root_in, 3)
            act.activation(small[:, 8:8 + NT], small[:, 4:4 + NT], ACT.Sqrt).then_inc(root_out, 1)
            act.wait_ge(rstd_ready, 1)
            for i in range(NT):
                for dst, done in ((n_tok, normed), (parts[0], part_ready[0])):
                    act.activation(dst[:, i, :], x_tok[:, i, :], ACT.Copy, scale=small[:, 32 + i:33 + i])\
                       .then_inc(done, 1)
            for i in range(NT):
                if i == NT - 1:
                    act.wait_ge(exp_in, 2)
                    act.activation(gexp, gexp, ACT.Exp).then_inc(exp_out, 1)
                    act.activation(dexp, dexp, ACT.Exp).then_inc(exp_out, 1)
                act.wait_ge(rest_ready, i + 1)
                act.activation(parts[1][:, i, :], n_tok[:, i, :], ACT.Copy).then_inc(part_ready[1], 1)

            def put_on_diagonals(j, column):
                for i in range(NT):
                    act.activation(diagonal[:, j, i * P:(i + 1) * P], ident[:, :], ACT.Copy, scale=column[:, i:i + 1])\
                       .then_inc(diagonal_ready, 1)

            act.wait_ge(slots_ready, 1)
            for c in range(2):
                put_on_diagonals(c, slot_f[:, c, :])
            for c in range(2):
                read_aux(aux("spread", c))
            act.wait_ge(coefs_ready, 1)
            for c in range(2):
                put_on_diagonals(2 + c, coef[c])
            for c in range(2):
                read_aux(aux("spread", 2 + c))

            act.wait_ge(tables_ready, 3)
            last_back = act.value_load(table[0:1, 3 * NE + 1:3 * NE + 2], min_val=NE // 2, max_val=MAX_ITEMS)

            def item(i, side, c):
                act.wait_ge(gate_up_done, i + 1)
                for second in range(2):
                    act.activation(sig[:, second * QE:(second + 1) * QE], gate_and_up(second)[0:T, :], ACT.Silu)\
                       .then_inc(sig_ready, 1)
                act.wait_ge(hid_turned, i + 1)
                act.activation(hidT.rearrange("p k t -> p (k t)"), HT, ACT.Copy).then_inc(hidT_ready, 1)
                if c is not None:
                    act.wait_ge(combined, c * NT + NT)
                act.wait_ge(down_done, i + 1)
                for h in range(2):
                    act.activation(y_hi[side * T:(side + 1) * T, h * HALF:(h + 1) * HALF],
                                   Y[h * T:(h + 1) * T, :], ACT.Copy).then_inc(y_hi_ready, 1)

            with act.Fori(0, NE // 2) as pair:
                for side in range(2):
                    n = act.value_load(table[0:1, bass.ds(pair * 2 + side, 1)], min_val=1, max_val=N // T)
                    first = act.value_load(table[0:1, bass.ds(pair * 2 + (side + NE), 1)], min_val=0,
                                           max_val=MAX_ITEMS - 1)
                    back_first = act.value_load(table[0:1, bass.ds(pair * 2 + (side + 2 * NE + 1), 1)], min_val=0,
                                                max_val=MAX_ITEMS - 1)
                    if side == 0:
                        with act.Fori(0, n) as j:
                            item(first + j, 0, back_first + j)
                    else:
                        item(first, 1, None)
                        with act.If(n > 1), act.Fori(1, n) as j:
                            item(first + j, 1, back_first + j)

            load_root_table(3)
            for i in range(NT):
                act.wait_ge(tile_added, last_back * NT + (NT + i + 1))
                if i:
                    act.wait_ge(ssq_ready, 2 * NT + i)
                act.activation(junk, x_tok[:, i, :], ACT.Square, accum_out=small[:, 16 + i:17 + i]).then_inc(ssq_ready, 1)
                act.wait_ge(root_in, 4 + i)
                act.activation(small[:, 24 + i:25 + i], small[:, 20 + i:21 + i], ACT.Sqrt).then_inc(root_out, 1)
            for i in range(NT):
                act.wait_ge(normed, 2 * NT + i + 1)
                dst = y_prompt[0, i * P:(i + 1) * P, :] if i < NP // P else y_sample.rearrange("s t d -> (s t) d")
                act.dma_start(dst, n_tok[:, i, :]).then_inc(y_out, 16)
            act.wait_ge(y_out, 16 * NT)
            act.wait_ge(stage_out[0], 48)
            act.wait_ge(stage_out[1], 32)

        @block.vector
        def _(dve):
            chain = [0]

            def link(ins):
                chain[0] += 1
                ins.then_inc(dve_chain, 1)
                dve.wait_ge(dve_chain, chain[0])

            def rms_scale(n_ssq, n_root, src, mid, root, inv):
                dve.wait_ge(ssq_ready, n_ssq)
                dve.tensor_scalar(mid, src, 1.0 / D, 1e-6, ALU.mult, ALU.add).then_inc(root_in, 1)
                dve.wait_ge(root_out, n_root)
                link(dve.reciprocal(inv, root))

            dve.wait_ge(x_in, 32)
            dve.scalar_tensor_tensor(cva[:, :, :].rearrange("p k n -> p (k n)")[:, (NT - 1) * D:NT * D],
                                     x_tok[:, NT - 1, :], 1.0, x_tok[:, NT - 1, :], ALU.mult, ALU.mult,
                                     accum_out=small[:, NT - 1:NT]).then_inc(ssq_ready, 1)
            rms_scale(NT, 1, small[:, 0:NT], small[:, 4:4 + NT], small[:, 8:8 + NT], small[:, 12:12 + NT])
            for i in range(NT):
                dve.tensor_scalar(n_tok[:, i, :], x_tok[:, i, :], small[:, 12 + i:13 + i], None, ALU.mult)\
                   .then_inc(normed, 1)

            def read_aux(a):
                name, j, eng = AUX[a]
                if eng != "dve":
                    return
                b = bank[4 + a % 4]
                dve.wait_ge(aux_done, a + 1)
                if name == "vec":
                    dve.tensor_copy(vec[:, :, :].rearrange("p k v -> p (k v)"), b[:, 0:KB * NV]).then_inc(dve_aux, 1)
                elif name == "xT":
                    dve.wait_ge(dve_aux, 1)
                    dve.wait_ge(x_hi_ready, j + 1)
                    dve.scalar_tensor_tensor(x_lo[:, j, :], b[:, 0:N], vec[:, j, V_N1:V_N1 + 1],
                                             x_hi[:, j, :].bitcast(F32), ALU.mult, ALU.subtract).then_inc(dve_aux, 1)
                elif name == "ca":
                    for m in range(KB):
                        dst = ua_k[:, m, PA:WA].rearrange("p (s n) -> p s n", s=NS)[:, :, 0:HA]
                        src = b[:, m * NS * HA:(m + 1) * NS * HA].rearrange("p (s n) -> p s n", s=NS)
                        last = dve.tensor_copy(dst, src)
                    last.then_inc(dve_aux, 1)
                elif name == "x2T":
                    t, h = j // 2, j % 2
                    dve.tensor_copy(x2T[:, 4 * h:4 * h + 4, t * P:(t + 1) * P],
                                    b[:, :].rearrange("p (k n) -> p k n", k=4)).then_inc(dve_aux, 1)

            for a in range(aux("ca")):
                read_aux(a)

            dve.wait_ge(consts, 13)
            dve.memset(own_slot[T:P, 0:1], -BIG).then_inc(own_slot_ready, 1)
            dve.memset(own_slot[0:T, 1:2], -BIG).then_inc(own_slot_ready, 1)
            odd = own_slot[T:P, 1:2]
            dve.tensor_scalar(odd, odd, -float(T), None, ALU.add).then_inc(own_slot_ready, 1)
            for g in range(P // TQ):
                own = own_slot[g * TQ:(g + 1) * TQ, 2:3]
                first_of = TQ if g < 2 else 0
                dve.tensor_scalar(own, own, float(first_of - g * TQ), None, ALU.add).then_inc(own_slot_ready, 1)

            conv_b_at = {}
            ops = [0]

            def conv_b(half, tap):
                for m in range(4 * half, 4 * half + 4):
                    w = vec[:, m, V_CB + tap:V_CB + tap + 1]
                    if half == 1 and tap == HEAD:
                        dve.wait_ge(product_added, product_number("b", m, HEAD - 1))
                    for part, (src, dst) in enumerate(zip(ub_new(m, tap), both(cvb[:, m, :]))):
                        if tap == 0:
                            ins = dve.tensor_scalar(dst, src, w, vec[:, m, V_CBB:V_CBB + 1], ALU.mult, ALU.add)
                        else:
                            if (m, part) in conv_b_at:
                                dve.wait_ge(conv_b_ops, conv_b_at[m, part])
                            ins = dve.scalar_tensor_tensor(dst, src, w, dst, ALU.mult, ALU.add)
                        ins.then_inc(conv_b_ops, 1)
                        ops[0] += 1
                        conv_b_at[m, part] = ops[0]

            def read_group(g):
                s, m, q = GROUPS[g]
                dve.wait_ge(grp_done, g + 1)
                b = bank[g % NBANK]
                if s == "GA":
                    wait_group_read(dve, group("GB", m))
                    for src, t, dst in zip(both(b[:, 0:N]), both(tmp[:, m % 4, :]), ub_new(m, HB)):
                        last = dve.tensor_tensor(dst, src, t, ALU.mult)
                    last.then_inc(dve_grp, 1)
                elif s == "H":
                    wait_group_read(dve, group("C", m))
                    for src, t, dst in zip(both(b[:, 0:N]), both(tmp[:, m % 4, :]), ua_new(m, HA)):
                        last = dve.tensor_tensor(dst, src, t, ALU.mult)
                    last.then_inc(dve_grp, 1)
                elif s == "B":
                    dve.wait_ge(product_added, product_number("a", m, KA_TAPS - 1))
                    dve.tensor_tensor(cva[:, m, :], b[:, 0:N], cva[:, m, :], ALU.mult).then_inc(dve_grp, 1)
                elif s == "Wb":
                    wait_group_read(dve, group("gB", m))
                    dve.wait_ge(gate_a_merged, m + 1)
                    dve.scalar_tensor_tensor(cva[:, m, :], b[:, 0:N], vec[:, m, V_BO:V_BO + 1], cva[:, m, :],
                                             ALU.add, ALU.mult).then_inc(dve_grp, 1)
                    wait_group_read(dve, g)
                    dve.tensor_tensor(merged[:, m, :], merged[:, m, :], cva[:, m, :], ALU.add).then_inc(added, 1)
                else:
                    half = q - (NCH - 2)
                    xs = x_tok[:, m, half * 512:(half + 1) * 512]
                    dve.tensor_tensor(xs, b[:, :], xs, ALU.add).then_inc(dve_grp, 1)

            taps = [(0, k) for k in range(KB_TAPS)] + [(1, k) for k in range(HEAD, KB_TAPS)]
            for q, (s, half) in enumerate(CHUNKS):
                groups = [i for i, x in enumerate(GROUPS) if x[2] == q]
                n_slices = SLICES.get(q, 0)
                for _ in range(min(2, n_slices)):
                    conv_b(*taps.pop(0))
                for j, g in enumerate(groups):
                    if s not in BY_ACT:
                        read_group(g)
                    if 2 + j < n_slices:
                        conv_b(*taps.pop(0))
                if q in (1, 3):
                    wait_group_read(dve, groups[-1])
                if q == 1:
                    read_aux(aux("ca"))
                    dve.wait_ge(hist_zero, 2)
                    for j in range(4):
                        wait_aux_read(dve, aux("cb", j))
                    wait_aux_read(dve, aux("ca"))
                if q == MEAN_AT:
                    assert not taps
                    dve.wait_ge(aux_done, aux("mean"))
                    for m, part in ((m, part) for m in range(KB) for part in range(2)):
                        dve.wait_ge(conv_b_ops, conv_b_at[m, part])
                    link(dve.tensor_tensor(sq[:, 0, :], cvb[:, 0, :], cvb[:, 1, :], ALU.add))
                    for k in range(2, KB):
                        last = dve.tensor_tensor(sq[:, 0, :], sq[:, 0, :], cvb[:, k, :], ALU.add)
                        if k < KB - 1:
                            link(last)
                    last.then_inc(blocks_summed, 1)
                    a = aux("mean")
                    dve.wait_ge(aux_done, a + 1)
                    for k in range(KB):
                        last = dve.scalar_tensor_tensor(cvb[:, k, :], bank[4 + a % 4][:, 0:N], -1.0 / D, cvb[:, k, :],
                                                        ALU.mult, ALU.add)
                        last.then_inc(centred, 1)
                    dve.wait_ge(centred, KB)
                    dve.tensor_copy(mark[:, 0:1], iota[:, 0:1]).then_inc(dve_aux, 1)
                if q == VAR_AT:
                    dve.wait_ge(squared, 1)
                    for k in range(1, KB):
                        dve.wait_ge(squared, k + 1)
                        last = dve.tensor_tensor(sq[:, 0, :], sq[:, 0, :], sq[:, k, :], ALU.add)
                        if k < KB - 1:
                            link(last)
                    last.then_inc(blocks_summed, 1)
                    a = aux("var")
                    dve.wait_ge(aux_done, a + 1)
                    dve.tensor_scalar(sq[:, 1, :], bank[4 + a % 4][:, 0:N], 1.0 / D, 1e-5, ALU.mult, ALU.add)\
                       .then_inc(dve_aux, 1)
                    wait_aux_read(dve, a)
                    dve.tensor_copy(mark[:, 1:2], iota[:, 0:1]).then_inc(root_in, 1)
                    dve.wait_ge(root_out, 2)
                    link(dve.reciprocal(sq[:, 2, :], sq[:, 0, :]))
                    for k in range(KB):
                        dve.tensor_tensor(cvb[:, k, :], cvb[:, k, :], sq[:, 2, :], ALU.mult).then_inc(scaled, 1)

            dve.wait_ge(rw_in, 64)
            link(dve.tensor_tensor(rw, rw, vec[:, :, V_N2:V_N2 + 1].to_broadcast([P, KB, R]), ALU.mult))
            dve.tensor_copy(mark[:, 2:3], iota[:, 0:1]).then_inc(rw_scaled, 1)
            for i in range(NT):
                read_aux(aux("x2T", 2 * i))
            dve.wait_ge(ssq_ready, 2 * NT)
            dve.tensor_scalar(small[:, 4:4 + NT], small[:, 0:NT], 1.0 / D, 1e-6, ALU.mult, ALU.add).then_inc(root_in, 1)
            dve.wait_ge(root_out, 3)
            dve.reciprocal(small[:, 32:32 + NT], small[:, 8:8 + NT]).then_inc(rstd_ready, 1)
            dve.wait_ge(rstd_ready, 1)

            for i in range(NT):
                a = aux("logit", i)
                dve.wait_ge(aux_done, a + 1)
                dve.scalar_tensor_tensor(lg[:, i, :], bank[4 + a % 4][:, 0:R], small[:, 32 + i:33 + i], rbias,
                                         ALU.mult, ALU.add).then_inc(dve_aux, 1)
            wait_aux_read(dve, aux("logit", NT - 1))

            def spread(col, n):
                return col.unsqueeze(2).to_broadcast([P, NT, n])

            def first_max(values, n, best, hot_out, ta):
                link(dve.tensor_reduce(best, values, AX.X, ALU.max))
                link(dve.tensor_tensor(ta, values, spread(best, n), ALU.is_equal))
                link(dve.tensor_tensor(ta, ta, down_rank[:, 0:n].unsqueeze(1).to_broadcast([P, NT, n]), ALU.mult))
                link(dve.tensor_reduce(psum_g, ta, AX.X, ALU.max))
                link(dve.tensor_tensor(hot_out, ta, spread(psum_g, n), ALU.is_equal))

            dve.wait_ge(consts, 13)
            first_max(lg[:, :, 0:NG], NG, gmax, ghot, t0[:, :, 0:NG])
            gpen = t1[:, :, 0:NG]
            link(dve.tensor_scalar(gpen, ghot, BIG, -BIG, ALU.mult, ALU.add))
            link(dve.tensor_tensor(le.rearrange("p i (g e) -> p i g e", g=NG),
                                   lg[:, :, NG:R].rearrange("p i (g e) -> p i g e", g=NG),
                                   gpen.unsqueeze(3).to_broadcast([P, NT, NG, EPG]), ALU.add))
            first_max(le, NE, top[0], hot[0], t0)
            link(dve.scalar_tensor_tensor(le, hot[0], -BIG, le, ALU.mult, ALU.add))
            first_max(le, NE, top[1], hot[1], t0)
            dve.tensor_tensor(both_b, hot[0], hot[1], ALU.add).then_inc(masks_ready, 1)
            dve.tensor_tensor(gexp, lg[:, :, 0:NG], spread(gmax, NG), ALU.subtract).then_inc(exp_in, 1)
            dve.tensor_tensor(dexp, top[1], top[0], ALU.subtract).then_inc(exp_in, 1)

            a = aux("pos")
            b = bank[4 + a % 4]
            dve.wait_ge(aux_done, a + 1)
            link(dve.tensor_copy(cnt, b[0:NE, NT * NE:NT * NE + 1]))
            link(dve.tensor_scalar(more_each, steps[:], cnt, None, ALU.is_lt))
            every_second = more_each[:, 1:N // TQ - 1].rearrange("e (n two) -> e n two", two=2)[:, :, 0]
            link(dve.tensor_reduce(more, every_second, AX.X, ALU.add))
            dve.tensor_scalar(ntile_b, ones[0:NE, :], more, 1.0, ALU.mult, ALU.add).then_inc(counts_ready, 1)
            dve.tensor_copy(t0, b[:, 0:NT * NE].rearrange("p (i e) -> p i e", i=NT)).then_inc(dve_aux, 1)
            a = aux("table")
            b = bank[4 + a % 4]
            dve.wait_ge(aux_done, a + 1)
            wait_aux_read(dve, aux("pos"))
            link(dve.scalar_tensor_tensor(t0, b[:, NE:2 * NE].unsqueeze(1).to_broadcast([P, NT, NE]), float(T), t0,
                                          ALU.mult, ALU.add))
            link(dve.tensor_tensor(hot_slots, hots, t0.unsqueeze(1).to_broadcast([P, 2, NT, NE]), ALU.mult))
            link(dve.tensor_reduce(slot_rem, hot_slots, AX.X, ALU.add))
            dve.tensor_copy(slot_f, slot_rem).then_inc(slots_ready, 1)
            dve.wait_ge(slots_ready, 1)

            def pick_tokens(pick_base, pick_n):
                for i in range(NT):
                    dve.tensor_scalar(pick[:, i, :], iota[:, :], slot_rem[:, 0, i:i + 1], None, ALU.is_equal)\
                       .then_inc(pick_half, 1)
                for i in range(NT):
                    dve.wait_ge(pick_half, pick_base + i + 1)
                    last = dve.scalar_tensor_tensor(pick[:, i, :], iota[:, :], slot_rem[:, 1, i:i + 1],
                                                    pick[:, i, :], ALU.is_equal, ALU.add)
                last.then_inc(picked, 1)
                dve.wait_ge(picked, pick_n + 1)
                dve.tensor_scalar(slot_rem, slot_rem, -float(T), None, ALU.add).then_inc(rem_ready, 1)
                dve.wait_ge(rem_ready, pick_n + 1)

            def take_gathered(n):
                dve.wait_ge(gathered, n)
                dve.tensor_tensor(xe, XE.rearrange("p (k t) -> p k t", k=KB),
                                  vec[:, :, V_N2:V_N2 + 1].to_broadcast([P, KB, T]), ALU.mult).then_inc(xe_ready, 1)

            pick_tokens(0, 0)
            link(dve.tensor_reduce(more, more_each, AX.X, ALU.add))
            dve.tensor_scalar(quarters_b, ones[0:NE, :], more, 1.0, ALU.mult, ALU.add).then_inc(counts_ready, 1)
            dve.wait_ge(part_ready[1], NT)
            dve.tensor_tensor(parts[2][:, NT - 1, :], n_tok[:, NT - 1, :], parts[1][:, NT - 1, :], ALU.subtract)\
               .then_inc(part_ready[2], 1)
            dve.tensor_copy(table[:, 0:2 * NE + 1], b[0:1, 0:2 * NE + 1]).then_inc(tables_ready, 1)
            dve.tensor_tensor(table[:, 2 * NE + 1:3 * NE + 2], b[0:1, NE:2 * NE + 1], pairs_before[:, 0:NE + 1],
                              ALU.subtract).then_inc(tables_ready, 1)
            dve.wait_ge(tables_ready, 2)
            a_q = aux("quarters")
            dve.wait_ge(aux_done, a_q + 1)
            dve.tensor_copy(table[:, 3 * NE + 2:], bank[4 + a_q % 4][0:1, 0:NE]).then_inc(tables_ready, 1)
            dve.wait_ge(tables_ready, 3)
            dve.tensor_copy(mark[:, 3:4], iota[:, 0:1]).then_inc(dve_aux, 1)
            dve.tensor_copy(mark[:, 4:5], iota[:, 0:1]).then_inc(dve_aux, 1)
            dve.wait_ge(exp_out, 2)
            link(dve.tensor_reduce(psum_g, gexp, AX.X, ALU.add))
            link(dve.tensor_scalar(coef[1], dexp, 1.0, None, ALU.add))
            link(dve.tensor_tensor(coef[1], coef[1], psum_g, ALU.mult))
            link(dve.reciprocal(coef[0], coef[1]))
            dve.tensor_tensor(coef[1], dexp, coef[0], ALU.mult).then_inc(coefs_ready, 1)

            def add_rows(c):
                for t in range(NT):
                    dve.wait_ge(combined, c * NT + t + 1)
                    dve.wait_ge(tile_added, c * NT + t + 1)
                    for h in range(2):
                        xs = x_tok[:, t, h * HALF:(h + 1) * HALF]
                        last = dve.tensor_tensor(xs, back(t)[h][:, :], xs, ALU.add)
                    last.then_inc(tile_added, 1)

            def next_coefficients(n):
                for c in range(2):
                    dve.scalar_tensor_tensor(at_slot[:, c, :], spread_rows[:, c, :], own_slot[:, 2:3],
                                             spread_rows[:, 2 + c, :], ALU.is_equal, ALU.mult,
                                             accum_out=coef_part[:, c:c + 1]).then_inc(coef_half, 1)
                dve.wait_ge(coef_half, n * 2 + 2)
                for second, found in enumerate((slice(T, P), slice(0, T))):
                    dve.tensor_tensor(slot_coef[T:P, second:second + 1], coef_part[found, 0:1],
                                      coef_part[found, 1:2], ALU.add).then_inc(slot_coef_ready, 1)

            dve.memset(gate_and_up(1), 0.0).then_inc(gate_up_clear, 1)
            take_gathered(1)
            pick_tokens(NT, 1)
            wait_aux_read(dve, aux("spread", 3))
            dve.tensor_copy(mark[:, 5:6], iota[:, 0:1]).then_inc(tile_added, NT)
            dve.wait_ge(own_slot_ready, OWN_FIRST)
            next_coefficients(0)

            def item(i, side, c):
                dve.wait_ge(slot_coef_ready, i * 2 + 2)
                for second in range(2):
                    cols = slice(second * QE, (second + 1) * QE)
                    dve.wait_ge(sig_ready, i * 2 + (second + 1))
                    last = dve.scalar_tensor_tensor(hid[:, cols], gate_and_up(second)[T:2 * T, :], slot_coef[T:2 * T, second:second + 1],
                                                    sig[:, cols], ALU.mult, ALU.mult)
                last.then_inc(hid_ready, 1)
                if c is not None:
                    add_rows(c)
                    take_gathered(i + 2)
                    pick_tokens(i * NT + 2 * NT, i + 2)
                mine = slice(T, 2 * T) if c is None else slice(0, 2 * T)
                own = own_slot[mine, side:side + 1]
                dve.wait_ge(own_slot_ready, i + OWN_FIRST)
                dve.tensor_scalar(at_slot[mine, 0, :], spread_rows[mine, 0, :], own, None, ALU.is_equal)\
                   .then_inc(back_part, 1)
                dve.wait_ge(back_part, i + 1)
                dve.scalar_tensor_tensor(back_to[mine, :], spread_rows[mine, 1, :], own, at_slot[mine, 0, :],
                                         ALU.is_equal, ALU.add).then_inc(back_ready, 1)
                dve.wait_ge(back_ready, i + 2)
                dve.tensor_scalar(own_slot[:], own_slot[:], float(T), None, ALU.add).then_inc(own_slot_ready, 1)
                dve.wait_ge(own_slot_ready, i + (OWN_FIRST + 1))
                next_coefficients(i + 1)
                if c is None:
                    take_gathered(i + 2)
                    pick_tokens(i * NT + 2 * NT, i + 2)
                for h in range(2):
                    dve.wait_ge(y_hi_ready, i * 2 + (h + 1))
                    cols = slice(h * HALF, (h + 1) * HALF)
                    rows = slice(side * T, (side + 1) * T)
                    last = dve.tensor_tensor(y_lo[rows, cols], Y[h * T:(h + 1) * T, :], y_hi[rows, cols].bitcast(F32),
                                             ALU.subtract)
                last.then_inc(y_ready, 1)

            with dve.Fori(0, NE // 2) as pair:
                for side in range(2):
                    n = dve.value_load(table[0:1, bass.ds(pair * 2 + side, 1)], min_val=1, max_val=N // T)
                    first = dve.value_load(table[0:1, bass.ds(pair * 2 + (side + NE), 1)], min_val=0,
                                           max_val=MAX_ITEMS - 1)
                    back_first = dve.value_load(table[0:1, bass.ds(pair * 2 + (side + 2 * NE + 1), 1)], min_val=0,
                                                max_val=MAX_ITEMS - 1)
                    if side == 0:
                        with dve.Fori(0, n) as j:
                            item(first + j, 0, back_first + j)
                    else:
                        item(first, 1, None)
                        with dve.If(n > 1), dve.Fori(1, n) as j:
                            item(first + j, 1, back_first + j)

            last_back = dve.value_load(table[0:1, 3 * NE + 1:3 * NE + 2], min_val=NE // 2, max_val=MAX_ITEMS)
            add_rows(last_back)
            def mean_square(i):
                dve.wait_ge(ssq_ready, 2 * NT + i + 1)
                dve.tensor_scalar(small[:, 20 + i:21 + i], small[:, 16 + i:17 + i], 1.0 / D, 1e-6, ALU.mult, ALU.add)\
                   .then_inc(root_in, 1)

            dve.wait_ge(g_in, 16)
            mean_square(0)
            for i in range(NT):
                dve.wait_ge(root_out, 4 + i)
                link(dve.reciprocal(small[:, 28 + i:29 + i], small[:, 24 + i:25 + i]))
                if i < NT - 1:
                    mean_square(i + 1)
                dve.scalar_tensor_tensor(n_tok[:, i, :], x_tok[:, i, :], small[:, 28 + i:29 + i], gf,
                                         ALU.mult, ALU.mult).then_inc(normed, 1)

        @block.tensor
        def _(pe):
            def start_aux(a):
                if a >= 4:
                    wait_aux_read(pe, a - 4)
                return bank[4 + a % 4]

            def end_aux(ins):
                ins.then_inc(aux_done, 1)

            pe.wait_ge(consts, 13)
            pe.wait_ge(vec_in, 16 * 9)
            b = start_aux(aux("vec"))
            for m in range(KB):
                last = pe.transpose(b[:, m * NV:(m + 1) * NV], stage[0:NV, 0, m * P:(m + 1) * P], ident[0:NV, 0:NV])
            end_aux(last)
            for k in range(KB):
                b = start_aux(aux("xT", k))
                for i in range(NT):
                    pe.wait_ge(normed, i + 1)
                    last = pe.transpose(b[:, i * P:(i + 1) * P], n_tok[:, i, k * P:(k + 1) * P], ident[:, :])
                end_aux(last)
            def cached_rows():
                pe.wait_ge(cache_in, 32)
                b = start_aux(aux("ca"))
                n = NS * HA
                for m in range(KB):
                    last = pe.transpose(b[:, m * n:(m + 1) * n], stage[0:n, 1, m * P:(m + 1) * P], ident[0:n, 0:n])
                end_aux(last)
                n = NS // 2 * HB
                cache_rows = cvb[:, :, :].rearrange("p k n -> p (k n)")[:, 0:2 * D].rearrange("p (t d) -> p t d", t=2)
                for j in range(4):
                    b = start_aux(aux("cb", j))
                    for m in range(4):
                        c0 = (4 * (j % 2) + m) * P
                        last = pe.transpose(b[:, m * n:(m + 1) * n], cache_rows[0:n, j // 2, c0:c0 + P], ident[0:n, 0:n])
                    end_aux(last)

            def new_rows(t, m):
                if t == 0:
                    return ua_k[:, m, PA - HA:PA]
                if t == 1:
                    return tails[:, m, 0:NS * HA]
                if t == 2:
                    return ub_k[:, m, PB - HB:PB]
                n = NS // 2 * HB
                return tails[:, m, NS * HA + (t - 3) * n:NS * HA + (t - 2) * n]

            def split_products(b, cols, w, x, k, first, last_of_group, weights_move):
                for n, (wp, xp) in enumerate(((w[0], x[0]), (w[0], x[1]), (w[1], x[0]))):
                    start, stop = first and n == 0, last_of_group and n == 2
                    if weights_move:
                        ins = pe.matmul(b, xp[:, k, cols], wp[:, k % UK, :], start=start, stop=stop)
                    else:
                        ins = pe.matmul(b, wp[:, k % UK, cols], xp[:, k, :], start=start, stop=stop)
                return ins

            for q, (s, half) in enumerate(CHUNKS):
                groups = [i for i, x in enumerate(GROUPS) if x[2] == q]
                for h in range(2):
                    u = 2 * q + h
                    pe.wait_ge(lo_ready, u + 1)
                    ready = {"Wa": (in_lo_ready, UK * (h + 1)), "Wb": (in_lo_ready, KB + UK * (h + 1)),
                             "Wo": (merged_lo_ready, UK * (h + 1))}.get(s)
                    if ready:
                        pe.wait_ge(*ready)
                    x = {"Wa": (in_hi, cva_lo), "Wb": (in_hi, cvb_lo), "Wo": (x_hi, merged_lo)}.get(s, (x_hi, x_lo))
                    for j, g in enumerate(groups):
                        if h == 0 and g >= NBANK:
                            wait_group_read(pe, g - NBANK)
                        b = bank[g % NBANK]
                        for kk in range(UK):
                            k = h * UK + kk
                            if q == 0 and j == 0:
                                wait_aux_read(pe, aux("xT", k))
                            last = split_products(b[:, :] if s == "Wo" else b[:, 0:N], slice(j * P, (j + 1) * P),
                                                  (w_hi[u % NW], w_lo[u % NW]), x, k, k == 0, k == KB - 1, s == "Wo")
                        if h == 1:
                            last.then_inc(grp_done, 1)
                    if h == 0:
                        last.then_inc(half_done, 1)
                    if (q, h) == (MEAN_AT, 0):
                        pe.wait_ge(blocks_summed, 1)
                        end_aux(pe.matmul(start_aux(aux("mean"))[:, 0:N], ones[:, :], sq[:, 0, :], start=True, stop=True))
                    if (q, h) == (VAR_AT, 0):
                        pe.wait_ge(blocks_summed, 2)
                        end_aux(pe.matmul(start_aux(aux("var"))[:, 0:N], ones[:, :], sq[:, 0, :], start=True, stop=True))
                if q == 1:
                    cached_rows()
                if q == NEW_AT:
                    pe.wait_ge(tails_ready, 2 * KB)
                    for a in range(aux("new", 0), aux("mean")):
                        t, h = AUX[a][1] // 2, AUX[a][1] % 2
                        b = start_aux(a)
                        for m4 in range(4):
                            last = pe.transpose(b[0:OUT_ROWS[t], m4 * P:(m4 + 1) * P], new_rows(t, 4 * h + m4),
                                                ident[:, :])
                        end_aux(last)

            for a in range(aux("x2T", 0), aux("logit", 0)):
                t, h = AUX[a][1] // 2, AUX[a][1] % 2
                b = start_aux(a)
                wait_group_read(pe, WO_LAST[t])
                for k in range(4):
                    last = pe.transpose(b[:, k * P:(k + 1) * P], x_tok[:, t, (4 * h + k) * P:(4 * h + k + 1) * P],
                                        ident[:, :])
                end_aux(last)
            pe.wait_ge(rw_scaled, 1)
            for i in range(NT):
                b = start_aux(aux("logit", i))
                for h in range(2):
                    wait_aux_read(pe, aux("x2T", 2 * i + h))
                for k in range(KB):
                    last = pe.matmul(b[:, 0:R], x2T[:, k, i * P:(i + 1) * P], rw[:, k, :],
                                     start=(k == 0), stop=(k == KB - 1))
                end_aux(last)
            pe.wait_ge(masks_ready, 1)
            b = start_aux(aux("pos"))
            for i in range(NT):
                for j in range(i + 1):
                    pe.matmul(b[:, i * NE:(i + 1) * NE], before_b[:, :] if j == i else ones_b[:, :], both_b[:, j, :],
                              start=(j == 0), stop=(j == i))
            for j in range(NT):
                last = pe.matmul(b[0:NE, NT * NE:NT * NE + 1], both_b[:, j, :], ones_b[:, 0:1],
                                 start=(j == 0), stop=(j == NT - 1))
            end_aux(last)
            pe.wait_ge(counts_ready, 1)
            b = start_aux(aux("table"))
            end_aux(pe.matmul(b[:, 0:2 * NE + 1], ntile_b, table_sums[:, :], start=True, stop=True))
            pe.wait_ge(counts_ready, 2)
            b = start_aux(aux("quarters"))
            end_aux(pe.matmul(b[:, 0:NE], quarters_b, table_sums[:, 0:NE], start=True, stop=True))

            def gather(blocks):
                for k in blocks:
                    for c in range(3):
                        for i in range(NT):
                            last = pe.matmul(XE[:, k * T:(k + 1) * T], parts[c][:, i, k * P:(k + 1) * P],
                                             pick[:, i, :], start=(c == 0 and i == 0), stop=(c == 2 and i == NT - 1))
                if KB - 1 in blocks:
                    last.then_inc(gathered, 1)

            def spread(j):
                pe.wait_ge(diagonal_ready, (j + 1) * NT)
                b = start_aux(aux("spread", j))
                end_aux(pe.matmul(b[:, 0:N], ones[:, :], diagonal[:, j, :], start=True, stop=True))

            spread(0)
            spread(1)
            pe.wait_ge(picked, 1)
            for part in part_ready:
                pe.wait_ge(part, NT)
            wait_group_read(pe, len(GROUPS) - 1)
            gather(range(KB))
            pe.wait_ge(tables_ready, 3)
            items = pe.value_load(table[0:1, 2 * NE:2 * NE + 1], min_val=NE, max_val=MAX_ITEMS)
            last_back = pe.value_load(table[0:1, 3 * NE + 1:3 * NE + 2], min_val=NE // 2, max_val=MAX_ITEMS)
            spread(2)
            spread(3)
            pe.wait_ge(gate_up_clear, 1)

            def combine(t, c):
                pe.wait_ge(tile_added, c * NT + (NT, NT - 1, NT + 1)[t])
                for h, b in enumerate(back(t)):
                    for part, y in enumerate((y_hi, y_lo)):
                        last = pe.matmul(b[:, :], back_to[:, t * P:(t + 1) * P], y[:, h * HALF:(h + 1) * HALF],
                                         start=(part == 0), stop=(part == 1))
                last.then_inc(combined, 1)

            def gate_up(part, slots, second):
                for k in range(part * KB // 2, (part + 1) * KB // 2):
                    for q in range(4):
                        last = pe.matmul(gate_and_up(second)[q * TQ:(q + 1) * TQ, :],
                                         xe[:, k, second * TQ:(second + 1) * TQ],
                                         wide(slots[q // 2])[:, k, q % 2 * QE:(q % 2 + 1) * QE],
                                         start=(k == 0), stop=(k == KB - 1))
                return last

            def item(i, slots, filled, c, second_slots):
                pe.wait_ge(xe_ready, i + 1)
                for part, done in enumerate((gate_up_half, gate_up_done)):
                    pe.wait_ge(weights_in[slots[0]][part], filled)
                    pe.wait_ge(weights_in[slots[1]][part], filled)
                    with pe.If(second_slots):
                        gate_up(part, slots, 1)
                    gate_up(part, slots, 0).then_inc(done, 1)
                pe.wait_ge(y_ready, i + 2)
                if c is not None:
                    pe.wait_ge(back_ready, i + 1)
                    combine(0, c)
                    combine(1, c)
                pe.wait_ge(picked, i + 2)
                early = 1 if c is not None else KB // 2 + 1
                gather(range(early))
                pe.wait_ge(hid_ready, i + 1)
                gather([early])
                turned = HT.rearrange("p (h c second t) -> p h c second t", h=2, c=HK // 2, second=2)
                for second in range(2):
                    for c2 in range(HK // 2):
                        at_col = second * QE + c2 * P
                        last = pe.transpose(turned[:, :, c2, second, :], hid[:, at_col:at_col + P], ident[0:T, 0:T])
                last.then_inc(hid_turned, 1)
                gather(range(early + 1, KB - 2))
                if c is not None:
                    combine(2, c)
                gather(range(KB - 2, KB))
                pe.wait_ge(hidT_ready, i + 1)
                for part, done in enumerate((down_half, down_done)):
                    pe.wait_ge(weights_in[slots[2]][part], filled)
                    for k in range(part * HK // 2, (part + 1) * HK // 2):
                        for h in range(2):
                            last = pe.matmul(Y[h * T:(h + 1) * T, :], hidT[:, k, :],
                                             deep(slots[2])[:, k, h * HALF:(h + 1) * HALF],
                                             start=(k == 0), stop=(k == HK - 1))
                    last.then_inc(done, 1)

            with pe.Fori(0, NE // 2) as pair:
                for par in range(2):
                    e = pair * 2 + par
                    n = pe.value_load(table[0:1, bass.ds(e, 1)], min_val=1, max_val=N // T)
                    first = pe.value_load(table[0:1, bass.ds(e + NE, 1)], min_val=0, max_val=MAX_ITEMS - 1)
                    slots = [3 * par + c for c in range(3)]
                    filled = pair * 16 + 16
                    back_first = pe.value_load(table[0:1, bass.ds(e + (2 * NE + 1), 1)], min_val=0,
                                               max_val=MAX_ITEMS - 1)
                    quarters = pe.value_load(table[0:1, bass.ds(e + (3 * NE + 2), 1)], min_val=1, max_val=N // TQ)
                    if par == 0:
                        with pe.Fori(0, n) as j:
                            item(first + j, slots, filled, back_first + j, quarters > j * 2 + 1)
                    else:
                        item(first, slots, filled, None, quarters > 1)
                        with pe.If(n > 1), pe.Fori(1, n) as j:
                            item(first + j, slots, filled, back_first + j, quarters > j * 2 + 1)
            pe.wait_ge(y_ready, items + 2)
            pe.wait_ge(back_ready, items + 1)
            for t in range(NT):
                combine(t, last_back)


_INS = ["x_prompt", "x_sample", "cache_conv_a", "cache_conv_b", "norm1_g", "w_in", "gate_b", "conv_a_w", "w_out_a",
        "conv_b_w", "conv_b_b", "ln_b_g", "ln_b_b", "w_out_b", "b_out_b", "w_o", "norm2_g", "router_group_w",
        "router_group_b", "router_expert_w", "router_expert_b", "exp_w_gate", "exp_w_up", "exp_w_down",
        "final_norm_g"]


def kernel(**inputs):
    import numpy as np
    import concourse.bacc as bacc
    from concourse.bass_utils import run_bass_kernel_spmd

    nc = bacc.Bacc("TRN2", target_bir_lowering=False, num_devices=1)
    arrays, args = {}, []
    for name in _INS:
        a = np.ascontiguousarray(inputs[name])
        arrays[f"in_{name}"] = a
        args.append(nc.dram_tensor(f"in_{name}", a.shape, mybir.dt.from_np(a.dtype), kind="ExternalInput").ap())
    xp, xs, ca, cb = (inputs[n].shape for n in _INS[:4])
    outs = [xp, xs, (ca[0], xp[0]) + tuple(ca[2:]), ca, (cb[0], xp[0]) + tuple(cb[2:]), cb]
    for i, shape in enumerate(outs):
        args.append(nc.dram_tensor(f"out_{i}", tuple(shape), F32, kind="ExternalOutput").ap())
    trunk_program(nc, *args)
    r = run_bass_kernel_spmd(nc, [arrays], core_ids=[0])
    return tuple(r.results[0][f"out_{i}"] for i in range(len(outs)))
```
